# Optimizing a Trainium2 kernel written in Bass

```python
import math
import jax, jax.numpy as jnp
from jax import lax
import numpy as np

D_MODEL = 1024
BATCH = 1
SEQ = 256
DEPTH = 1

MEM_LEN = 256
ATT_HEADS = 8
ATT_HEAD_DIM = 64
ATT_WIDTH = ATT_HEADS * ATT_HEAD_DIM
MOBA_BLOCK = 256
MOBA_TOPK = 3
QUERY_CHUNK = 32
REL_BUCKETS = 32
REL_MAX_DIST = 128
CONV_WIDTH = D_MODEL // 2
CONV_K = 3
XATT_HEADS = 4
XATT_HEAD_DIM = 128
XATT_WIDTH = XATT_HEADS * XATT_HEAD_DIM
N_BRANCH = 3
N_EXPERTS = 32
TOP_K = 4
D_EXPERT = D_MODEL
SWIGLU_LIMIT = 7.0
SWIGLU_ALPHA = 1.702
ROUTE_BLOCK = 128
EPS = 1e-5
NEG = -1e30

IN_COLS = 3 * ATT_WIDTH + 3 * CONV_WIDTH + XATT_WIDTH + N_BRANCH * D_MODEL

kernel_name = "hybrid_moba_shortconv_xattn_moe"

def rmsnorm(x, g):
    xf = x.astype(jnp.float32)
    y = xf * lax.rsqrt(jnp.mean(xf * xf, axis=-1, keepdims=True) + EPS)
    return (y * g.astype(jnp.float32)).astype(x.dtype)

def t5_bucket(dist):
    n = jnp.maximum(dist, 0)
    max_exact = REL_BUCKETS // 2
    nf = jnp.maximum(n, 1).astype(jnp.float32)
    large = max_exact + (jnp.log(nf / max_exact) / math.log(REL_MAX_DIST / max_exact)
                         * (REL_BUCKETS - max_exact)).astype(jnp.int32)
    large = jnp.minimum(large, REL_BUCKETS - 1)
    return jnp.where(n < max_exact, n, large)

def moba_attention(q, k, v, rel_table):
    B, S, H, Dh = q.shape
    L = MOBA_BLOCK
    nb = -(-S // L)
    pad = nb * L - S
    kp = jnp.pad(k, ((0, 0), (0, pad), (0, 0), (0, 0)))
    vp = jnp.pad(v, ((0, 0), (0, pad), (0, 0), (0, 0)))
    kb = kp.reshape(B, nb, L, H, Dh).transpose(0, 3, 1, 2, 4)
    vb = vp.reshape(B, nb, L, H, Dh).transpose(0, 3, 1, 2, 4)
    k_mean = jnp.mean(kb.astype(jnp.float32), axis=3)
    qh = q.transpose(0, 2, 1, 3) * (1.0 / math.sqrt(Dh))
    n_sel = min(MOBA_TOPK, nb)
    bi = jnp.arange(B)[:, None, None, None]
    hi = jnp.arange(H)[None, :, None, None]
    blk_ids = jnp.arange(nb)
    offs = jnp.arange(L)

    def chunk_fn(c):
        start = c * QUERY_CHUNK
        qc = lax.dynamic_slice_in_dim(qh, start, QUERY_CHUNK, axis=2)
        q_pos = start + jnp.arange(QUERY_CHUNK)
        blk = start // L
        gate = jnp.einsum('bhqd,bhnd->bhqn', qc.astype(jnp.float32), k_mean)
        gate = jnp.where(blk_ids < blk, gate, -jnp.inf)
        _, sel = lax.top_k(gate, n_sel)
        sel_valid = sel < blk
        ks = kb[bi, hi, sel]
        vs = vb[bi, hi, sel]
        s_sel = jnp.einsum('bhqd,bhqnld->bhqnl', qc, ks).astype(jnp.float32)
        k_pos_sel = sel[..., None] * L + offs
        bias_sel = rel_table[t5_bucket(q_pos[:, None, None] - k_pos_sel), hi[..., None]]
        s_sel = jnp.where(sel_valid[..., None], s_sel + bias_sel.astype(jnp.float32), NEG)
        ko = lax.dynamic_index_in_dim(kb, blk, axis=2, keepdims=False)
        vo = lax.dynamic_index_in_dim(vb, blk, axis=2, keepdims=False)
        s_own = jnp.einsum('bhqd,bhld->bhql', qc, ko).astype(jnp.float32)
        dist = q_pos[:, None] - (blk * L + offs)[None, :]
        bias_own = rel_table[t5_bucket(dist)].transpose(2, 0, 1)
        s_own = jnp.where(dist >= 0, s_own + bias_own.astype(jnp.float32), NEG)
        logits = jnp.concatenate([s_sel.reshape(B, H, QUERY_CHUNK, n_sel * L), s_own], axis=-1)
        p = jax.nn.softmax(logits, axis=-1).astype(v.dtype)
        p_sel = p[..., :n_sel * L].reshape(B, H, QUERY_CHUNK, n_sel, L)
        p_own = p[..., n_sel * L:]
        return (jnp.einsum('bhqnl,bhqnld->bhqd', p_sel, vs)
                + jnp.einsum('bhql,bhld->bhqd', p_own, vo))

    outs = lax.map(chunk_fn, jnp.arange(S // QUERY_CHUNK))
    return outs.transpose(1, 0, 3, 2, 4).reshape(B, S, H * Dh)

def short_conv(b_gate, c_gate, u, conv_w):
    z = c_gate * u
    y = lax.conv_general_dilated(z, conv_w[:, None, :].astype(z.dtype), window_strides=(1,),
                                 padding=[(CONV_K - 1, 0)],
                                 dimension_numbers=('NWC', 'WIO', 'NWC'),
                                 feature_group_count=CONV_WIDTH)
    return b_gate * y

def memory_cross_attention(q, mem_n, w_mem_kv):
    B, S = q.shape[:2]
    kv = mem_n @ w_mem_kv
    k = kv[..., :XATT_WIDTH].reshape(B, -1, XATT_HEADS, XATT_HEAD_DIM)
    v = kv[..., XATT_WIDTH:].reshape(B, -1, XATT_HEADS, XATT_HEAD_DIM)
    s = jnp.einsum('bshd,bmhd->bhsm', q, k).astype(jnp.float32) * (1.0 / math.sqrt(XATT_HEAD_DIM))
    p = jax.nn.softmax(s, axis=-1).astype(v.dtype)
    return jnp.einsum('bhsm,bmhd->bshd', p, v).reshape(B, S, XATT_WIDTH)

def moe_ffn(h, w_router, b_router, w_gu, b_gu, w_down, b_down):
    B, S, D = h.shape
    T = B * S
    hf = h.reshape(T, D)
    logits = (hf @ w_router).astype(jnp.float32) + b_router.astype(jnp.float32)
    top_logit, top_idx = lax.top_k(logits, TOP_K)
    top_w = jax.nn.softmax(top_logit, axis=-1)
    flat_e = top_idx.reshape(-1)
    flat_tok = jnp.arange(T * TOP_K, dtype=jnp.int32) // TOP_K
    flat_w = top_w.reshape(-1)
    order = jnp.argsort(flat_e)
    sorted_e = flat_e[order]
    sorted_tok = flat_tok[order]
    sorted_w = flat_w[order]
    counts = jnp.bincount(flat_e, length=N_EXPERTS)
    starts = jnp.cumsum(counts) - counts
    padded = (counts + ROUTE_BLOCK - 1) // ROUTE_BLOCK * ROUTE_BLOCK
    pad_ends = jnp.cumsum(padded)
    pad_starts = pad_ends - padded
    dest = pad_starts[sorted_e] + (jnp.arange(T * TOP_K) - starts[sorted_e])
    n_rows = T * TOP_K + N_EXPERTS * ROUTE_BLOCK
    row_tok = jnp.full((n_rows,), T, jnp.int32).at[dest].set(sorted_tok)
    row_w = jnp.zeros((n_rows,), jnp.float32).at[dest].set(sorted_w)
    n_blocks = n_rows // ROUTE_BLOCK
    block_expert = jnp.minimum(
        jnp.searchsorted(pad_ends, jnp.arange(n_blocks) * ROUTE_BLOCK, side='right'),
        N_EXPERTS - 1)
    hpad = jnp.concatenate([hf, jnp.zeros((1, D), hf.dtype)], axis=0)
    xs = hpad[row_tok].reshape(n_blocks, ROUTE_BLOCK, D)

    def expert_block(args):
        xb, e = args
        gu = xb @ w_gu[e] + b_gu[e]
        g = jnp.minimum(gu[:, :D_EXPERT], SWIGLU_LIMIT)
        lin = jnp.clip(gu[:, D_EXPERT:], -SWIGLU_LIMIT, SWIGLU_LIMIT)
        glu = g * jax.nn.sigmoid(SWIGLU_ALPHA * g)
        return ((lin + 1.0) * glu) @ w_down[e] + b_down[e]

    ys = lax.map(expert_block, (xs, block_expert)).reshape(n_rows, D)
    ys = ys * row_w[:, None].astype(ys.dtype)
    out = jax.ops.segment_sum(ys, row_tok, num_segments=T + 1)[:T]
    return out.reshape(B, S, D)

def setup_inputs(seed: int = 0) -> dict:
    key = jax.random.key(seed)
    ks = jax.random.split(key, 24)
    f32 = jnp.float32
    L = DEPTH

    def nrm(k, shape, fan_in):
        return jax.random.normal(k, shape, f32) * (fan_in ** -0.5)

    def gain(k, shape):
        return 1.0 + 0.05 * jax.random.normal(k, shape, f32)

    return {
        "x": jax.random.normal(ks[0], (BATCH, SEQ, D_MODEL), f32),
        "mem": jax.random.normal(ks[1], (BATCH, MEM_LEN, D_MODEL), f32),
        "rel_bias": 0.3 * jax.random.normal(ks[2], (REL_BUCKETS, ATT_HEADS), f32),
        "norm_mix_g": gain(ks[3], (L, D_MODEL)),
        "w_in": nrm(ks[4], (L, D_MODEL, IN_COLS), D_MODEL),
        "b_gate": 0.1 * jax.random.normal(ks[5], (L, N_BRANCH, D_MODEL), f32),
        "conv_w": nrm(ks[6], (L, CONV_K, CONV_WIDTH), CONV_K),
        "norm_mem_g": gain(ks[7], (L, D_MODEL)),
        "w_mem_kv": nrm(ks[8], (L, D_MODEL, 2 * XATT_WIDTH), D_MODEL),
        "w_br_att": nrm(ks[9], (L, ATT_WIDTH, D_MODEL), ATT_WIDTH),
        "w_br_conv": nrm(ks[10], (L, CONV_WIDTH, D_MODEL), CONV_WIDTH),
        "w_br_xatt": nrm(ks[11], (L, XATT_WIDTH, D_MODEL), XATT_WIDTH),
        "w_out": nrm(ks[12], (L, D_MODEL, D_MODEL), D_MODEL),
        "norm_ffn_g": gain(ks[13], (L, D_MODEL)),
        "w_router": nrm(ks[14], (L, D_MODEL, N_EXPERTS), D_MODEL),
        "b_router": 0.01 * jax.random.normal(ks[15], (L, N_EXPERTS), f32),
        "w_gu": nrm(ks[16], (L, N_EXPERTS, D_MODEL, 2 * D_EXPERT), D_MODEL),
        "b_gu": 0.01 * jax.random.normal(ks[17], (L, N_EXPERTS, 2 * D_EXPERT), f32),
        "w_down": nrm(ks[18], (L, N_EXPERTS, D_EXPERT, D_MODEL), D_EXPERT),
        "b_down": 0.01 * jax.random.normal(ks[19], (L, N_EXPERTS, D_MODEL), f32),
        "norm_final_g": gain(ks[20], (D_MODEL,)),
    }

def reference(x, mem, rel_bias, norm_mix_g, w_in, b_gate, conv_w, norm_mem_g, w_mem_kv,
              w_br_att, w_br_conv, w_br_xatt, w_out, norm_ffn_g, w_router, b_router,
              w_gu, b_gu, w_down, b_down, norm_final_g):
    B, S, D = x.shape
    split_at = np.cumsum([ATT_WIDTH, ATT_WIDTH, ATT_WIDTH, CONV_WIDTH, CONV_WIDTH, CONV_WIDTH,
                          XATT_WIDTH]).tolist()
    for l in range(DEPTH):
        h = rmsnorm(x, norm_mix_g[l])
        proj = h @ w_in[l]
        qa, ka, va, cb, cc, cu, qx, glog = jnp.split(proj, split_at, axis=-1)
        shp_a = (B, S, ATT_HEADS, ATT_HEAD_DIM)
        y_att = moba_attention(qa.reshape(shp_a), ka.reshape(shp_a), va.reshape(shp_a), rel_bias)
        y_conv = short_conv(cb, cc, cu, conv_w[l])
        mem_n = rmsnorm(mem, norm_mem_g[l])
        y_xatt = memory_cross_attention(qx.reshape(B, S, XATT_HEADS, XATT_HEAD_DIM), mem_n, w_mem_kv[l])
        gates = jax.nn.sigmoid(glog.reshape(B, S, N_BRANCH, D) + b_gate[l])
        merged = (gates[:, :, 0] * (y_att @ w_br_att[l])
                  + gates[:, :, 1] * (y_conv @ w_br_conv[l])
                  + gates[:, :, 2] * (y_xatt @ w_br_xatt[l]))
        x = x + merged @ w_out[l]
        h2 = rmsnorm(x, norm_ffn_g[l])
        x = x + moe_ffn(h2, w_router[l], b_router[l], w_gu[l], b_gu[l], w_down[l], b_down[l])
    return rmsnorm(x, norm_final_g)


_drawn_inputs = setup_inputs


def setup_inputs(seed=0):
    import zlib

    import numpy as np

    out = dict(_drawn_inputs(seed))
    spreads = {}
    factors = {'norm_mem_g': 3.748, 'b_router': 3.136, 'b_gu': 8.0, 'b_down': 8.0}
    for name, (base, spread) in spreads.items():
        noise = np.random.default_rng([zlib.crc32(name.encode()), seed]).standard_normal(out[name].shape)
        drawn = base * np.exp(spread * noise) if base else spread * noise
        out[name] = __import__('jax').numpy.asarray(drawn.astype(out[name].dtype))
    for name, factor in factors.items():
        out[name] = (out[name] * factor).astype(out[name].dtype)
    return out
```

```python
import concourse.bass as bass
from concourse import mybir
import numpy as np
import math
from contextlib import ExitStack

P = 128
D = 1024
S = 256
M = 256
ATT_H, ATT_D = 8, 64
X_H, X_D = 4, 128
CONV = 512
E = 32
TOPK = 4
BUCKETS = 32
MAX_DIST = 128
EPS = 1e-5
NEG = -1e30
LIMIT = 7.0
ALPHA = 1.702
F = D
KC = D // P
TT = S // P
SLOTS = 64
PASSES = S // SLOTS
STEPS = PASSES * E
TOEP = 3 * P - 1
RING = 16
PIECE = 2048
DRING = 4
IN_ORDER = 4

QA, KA, VA, CB, CC, CU, QX, GL = 0, 512, 1024, 1536, 2048, 2560, 3072, 3584
PROJ = ([("w_in", QA), ("w_in", QA + 256), ("w_in", KA), ("w_in", KA + 256),
         ("w_in", VA), ("w_in", VA + 256),
         ("w_in", CC), ("w_in", CC + 256), ("w_in", CU), ("w_in", CU + 256),
         ("w_in", CB), ("w_in", CB + 256), ("w_in", QX), ("w_in", QX + 256)]
        + [("w_mem_kv", 256 * j) for j in range(4)])
BRANCHES = [(1, "w_br_conv"), (0, "w_br_att"), (2, "w_br_xatt")]
GROUPS = [(b, w, half) for b, w in BRANCHES for half in range(2)]
N_PROJ = len(PROJ)
N_MIX = N_PROJ + 3 * len(GROUPS) + 4
HEADS = ATT_H + X_H


C_ID, C_TRI, C_SLOT, C_HALF, C_PICK = 0, P, 2 * P, 3 * P, 4 * P
C_KEPT = C_PICK + STEPS + 1


def shape_constants():
    c = np.zeros((P, C_KEPT + P), np.float32)
    r = np.arange(P)
    c[:, C_ID:C_ID + P] = np.eye(P)
    c[:, C_TRI:C_TRI + P] = np.triu(np.ones((P, P)), 1)
    c[:, C_SLOT:C_SLOT + P] = np.tile(np.arange(SLOTS), 2)[None]
    c[:, C_HALF:C_HALF + P] = (r[:, None] % (2 * E) // E) == (r[None] // SLOTS)
    c[:, C_PICK:C_KEPT] = (r[:, None] % E) == (np.arange(STEPS + 1)[None] % E)
    c[:, C_KEPT:] = np.eye(P)[::-1]
    hot = np.zeros((BUCKETS + 1, TOEP), np.float32)
    exact = BUCKETS // 2
    for i in range(TOEP):
        dist = 2 * P - 1 - i
        if dist < 0:
            hot[BUCKETS, i] = 1.0
        elif dist < exact:
            hot[dist, i] = 1.0
        else:
            large = exact + int(math.log(dist / exact) / math.log(MAX_DIST / exact) * (BUCKETS - exact))
            hot[min(large, BUCKETS - 1), i] = 1.0
    return c, hot


def trunk_layer(nc, a, out, scratch):
    ctx = ExitStack()
    with ctx:
        build(nc, a, out, scratch, ctx)


def build(nc, a, out, scratch, ctx):
    fp32 = mybir.dt.float32
    fp32r = mybir.dt.float32r
    i32 = mybir.dt.int32
    u32 = mybir.dt.uint32
    ALU = mybir.AluOpType
    ACT = mybir.ActivationFunctionType
    AX = mybir.AxisListType

    def sb(name, shape, dt=fp32):
        return nc.alloc_sbuf_tensor(name, shape, dt)

    ring = sb("ring", [P, RING, PIECE])
    dring = sb("dring", [P, DRING, PIECE])
    region_x = sb("region_x", [P, 2048])
    region_h = sb("region_h", [P, 2048])
    region_r = sb("region_r", [P, 6152])
    r_at = nc.sbuf_base - 4 * 6152

    def in_region_r(name, shape, at):
        return nc.alloc_sbuf_tensor_at(name, shape, fp32r, offset=r_at + 4 * at)

    scaT = in_region_r("scaT", [P, TT, P], 5000)
    sel = in_region_r("sel", [P, P], 5256)
    b_parts = in_region_r("b_parts", [P, 1024], 0)
    y_parts = sb("y_parts", [P, 1024], fp32r)
    consts = sb("consts", [P, C_KEPT])
    ones = sb("ones", [P, P])
    cols = sb("cols", [P, 60])
    zero = sb("zero", [P, 2])
    stats = sb("stats", [P, 3, HEADS, 2])
    norm = sb("norm", [P, 4, 8])
    more_i32 = sb("more_i32", [1, 1], i32)
    best_u = sb("best_u", [P, TT, 8], u32)

    ident = consts[:, C_ID:C_ID + P]
    before = consts[:, C_TRI:C_TRI + P]
    slot_no = consts[:, C_SLOT:C_SLOT + P]
    half_of = consts[:, C_HALF:C_HALF + P]
    pick = consts[:, C_PICK:C_KEPT]
    g_mix, g_mem, g_ffn = cols[:, 0:8], cols[:, 8:16], cols[:, 16:24]
    b_gate = cols[:, 24:48]
    conv_w = cols[:, 48:60]
    top, negtop, sums = stats[:, 0], stats[:, 1], stats[:, 2]

    hT = dring[:, 0, :].rearrange("p (c t) -> p c t", c=KC)
    memT = dring[:, 1, :].rearrange("p (c t) -> p c t", c=KC)
    qk = dring[:, 2, :].rearrange("p (c t) -> p c t", c=8)
    mem_nat = dring[:, 3, :].rearrange("p (t d) -> p t d", t=TT)
    merged = dring[:, 3, :].rearrange("p (c t) -> p c t", c=KC)
    x_nat = region_x[:, :].rearrange("p (t d) -> p t d", t=TT)
    qx = region_x[:, 0:1024].rearrange("p (c t) -> p c t", c=X_H)
    kx = region_x[:, 1024:2048].rearrange("p (c t) -> p c t", c=X_H)
    x2 = x_nat
    probs = [region_h[:, 512 * n:512 * n + 512] for n in range(2)]
    probsT = [region_h[:, 1024 + 512 * n:1024 + 512 * n + 512] for n in range(2)]
    squares = region_h[:, :].rearrange("p (t d) -> p t d", t=TT)
    x_again = squares
    h2 = squares
    bias = region_r[:, 0:2048].rearrange("p (h k) -> p h k", h=ATT_H)
    v_att = region_r[:, 2048:3072].rearrange("p (t c) -> p t c", t=TT)
    y_conv = region_r[:, 3072:4096].rearrange("p (c t) -> p c t", c=4)
    z = region_r[:, 4096:4096 + 4 * (S + 2)].rearrange("p (c t) -> p c t", c=4)
    vx = region_r[:, 4096:5120].rearrange("p (t c) -> p t c", t=TT)
    flip = region_r[:, 3072:3072 + P]
    sig = region_r[:, 5128:5640]
    prod = region_r[:, 5640:6152]
    rows = region_r[0:60, 5128:5256]
    table_hot = region_r[0:BUCKETS + 1, 5256:5264 + TOEP]
    table, hot = table_hot[:, 0:ATT_H], table_hot[:, ATT_H:]
    bias_of_dist = region_r[0:ATT_H, 5650:5650 + TOEP]
    squares2 = region_r[:, 2048:4096].rearrange("p (t d) -> p t d", t=TT)

    b_gu = region_r[:, 0:1024]
    b_down = region_r[0:E, 1024:2048]
    hidT = region_r[:, 1024:1536]
    xg = region_r[:, 2048:2560].rearrange("p (c s) -> p c s", c=KC)
    g_sb = region_r[:, 2560:3072]
    sg = region_r[:, 3072:3584]
    hid = region_r[:, 3584:4096]
    h2T = region_r[:, 2048:4096].rearrange("p (c t) -> p c t", c=KC)
    place = region_r[:, 4096:4096 + 2 * (STEPS + 1)].rearrange("p (t s) -> p t s", t=TT)
    wexp = region_r[:, 4354:4354 + 2 * (STEPS + 1)].rearrange("p (t s) -> p t s", t=TT)
    gat = region_r[:, 4612:4612 + TT * SLOTS].rearrange("p (t s) -> p t s", t=TT)
    sca = region_r[:, 4740:4740 + TT * P].rearrange("p (t s) -> p t s", t=TT)
    w_slot = region_r[:, 6132:6133]
    unused = region_r[:, 1536:1536 + TT * P]
    logit = region_r[:, 5316:5380].rearrange("p (t e) -> p t e", t=TT)
    mask = region_r[:, 5380:5444].rearrange("p (t e) -> p t e", t=TT)
    hit = region_r[:, 5444:5476]
    best = region_r[:, 5476:5492].rearrange("p (t k) -> p t k", t=TT)
    best_i = region_r[:, 5492:5508].rearrange("p (t k) -> p t k", t=TT)
    elog = region_r[:, 4612:4676].rearrange("p (t e) -> p t e", t=TT)
    gain_out = ring[:, 8, 0:D]
    rank = region_r[:, 5508:5572].rearrange("p (t e) -> p t e", t=TT)
    small = region_r[:, 5572:5588]
    w_rt = region_r[:, 5588:5844].rearrange("p (c e) -> p c e", c=KC)
    b_rt = region_r[:, 5844:5876]
    wexpT = region_r[0:E, 5876:6132]

    bank = [nc.alloc_psum_tensor(f"bank{n}", [P, 512], fp32) for n in range(8)]
    acc = [bank[0:2], bank[2:4]]
    gate_ps, lin_ps, tr_ps, y_ps = bank[4], bank[5], bank[6], bank[7]

    def sem(name):
        return ctx.enter_context(nc.semaphore(name))

    x_in = [sem(f"x_in{t}") for t in range(TT)]
    mem_in = [sem(f"mem_in{t}") for t in range(TT)]
    table_in, rows_in, bias_in, scratch_out = sem("table_in"), sem("rows_in"), sem("bias_in"), sem("scratch_out")
    x_again_in, expert_bias_in, router_in = sem("x_again_in"), sem("expert_bias_in"), sem("router_in")
    final_gain_in, out_done = sem("final_gain_in"), sem("out_done")
    piece_in = [sem(f"piece_in{n}") for n in range(RING)]
    down_in = [sem(f"down_in{n}") for n in range(DRING)]
    pieces_used, downs_used = sem("pieces_used"), sem("downs_used")
    cols_done, dist_done, bias_flipped = sem("cols_done"), sem("dist_done"), sem("bias_flipped")
    hT_done, scores_done = sem("hT_done"), sem("scores_done")
    probsT_done, pv_done, branch_done = sem("probsT_done"), sem("pv_done"), sem("branch_done")
    h2T_done, logits_done, rank_done = sem("h2T_done"), sem("logits_done"), sem("rank_done")
    wexpT_done, acc_open, acc_done = sem("wexpT_done"), sem("acc_open"), sem("acc_done")
    gathered, scaT_done, hidT_done, scattered = sem("gathered"), sem("scaT_done"), sem("hidT_done"), sem("scattered")
    cols_sb, dist_sb, mean_done, normed = sem("cols_sb"), sem("dist_sb"), sem("mean_done"), sem("normed")
    bias_sb = sem("bias_sb")
    hT_sb, proj_sb, att_scores_read, top_ready = sem("hT_sb"), sem("proj_sb"), sem("att_scores_read"), sem("top_ready")
    probs_ready, merged_sb, x2_sb, h2_sb, h2T_sb = sem("probs_ready"), sem("merged_sb"), sem("x2_sb"), sem("h2_sb"), sem("h2T_sb")
    best_ready, mask_sb, weights_sb, wexpT_sb = sem("best_ready"), sem("mask_sb"), sem("weights_sb"), sem("wexpT_sb")
    passes_ready = sem("passes_ready")
    gat_ready, sca_ready, sel_ready, xg_sb = sem("gat_ready"), sem("sca_ready"), sem("sel_ready"), sem("xg_sb")
    g_ready, up_read, hid_half, hid_ready = sem("g_ready"), sem("up_read"), sem("hid_half"), sem("hid_ready")
    b_parts_ready, scaT_sb, y_ready = sem("b_parts_ready"), sem("scaT_sb"), sem("y_ready")
    sum_ready, fin_sb, dve_step = sem("sum_ready"), sem("fin_sb"), sem("dve_step")
    sq_done, root_done, exp_done, probsT_sb = sem("sq_done"), sem("root_done"), sem("exp_done"), sem("probsT_sb")
    y_att_sb, gates_sb, router_exp = sem("y_att_sb"), sem("gates_sb"), sem("router_exp")
    sig_ready, hidT_sb, w_slot_ready, y_high = sem("sig_ready"), sem("hidT_sb"), sem("w_slot_ready"), sem("y_high")

    block = ctx.enter_context(nc.Block())

    @block.sync
    def _(sp):
        def mixer_piece(p, src, chunks):
            if p >= RING:
                sp.wait_ge(pieces_used, p - RING + 1)
            dst = ring[:, p % RING, :].rearrange("p (c n) -> p c n", c=chunks)
            sp.dma_start(dst, src).then_inc(piece_in[p % RING], 16)

        sp.dma_start(table_hot, a["table_hot"]).then_inc(table_in, 16)
        sp.dma_start(x_nat[:, 0, :], a["x"][0, 0:P, :]).then_inc(x_in[0], 16)
        sp.dma_start(x_nat[:, 1, :], a["x"][0, P:2 * P, :]).then_inc(x_in[1], 16)
        sp.dma_start(rows, a["rows"]).then_inc(rows_in, 16)
        sp.dma_start(consts[:, :], a["consts"][:, 0:C_KEPT]).then_inc(rows_in, 16)
        sp.dma_start(flip, a["consts"][:, C_KEPT:]).then_inc(rows_in, 16)
        p = 0
        for name, col in PROJ:
            if p == 4:
                sp.wait_ge(bias_in, 16)
                for t in range(TT):
                    sp.dma_start(mem_nat[:, t, :], a["mem"][0, t * P:(t + 1) * P, :]).then_inc(mem_in[t], 16)
            mixer_piece(p, a[name][0, :, col:col + 256].rearrange("(c p) n -> p c n", p=P), KC)
            p += 1
        for b, name, half in GROUPS:
            for j in range(2):
                col = GL + b * D + half * 512 + j * 256
                mixer_piece(p, a["w_in"][0, :, col:col + 256].rearrange("(c p) n -> p c n", p=P), KC)
                p += 1
            mixer_piece(p, a[name][0, :, half * 512:half * 512 + 512].rearrange("(c p) n -> p c n", p=P), 4)
            p += 1
        for j in range(4):
            mixer_piece(p, a["w_out"][0, j * 256:(j + 1) * 256, :].rearrange("(c p) n -> p c n", p=P), 2)
            p += 1
        sp.wait_ge(y_att_sb, ATT_H // 2 + X_H)
        sp.dma_start(x_again, a["x"][0].rearrange("(t p) d -> p t d", p=P)).then_inc(x_again_in, 16)

        def expert_up(expert, slot0, uses):
            for c in range(KC):
                sp.wait_ge(pieces_used, uses + c)
                sp.dma_start(ring[:, slot0 + c, :],
                             a["w_gu"][0, bass.ds(expert, 1), c * P:(c + 1) * P, :].rearrange("e p n -> (e p) n"))\
                  .then_inc(piece_in[slot0 + c], 16)

        def expert_down(expert, uses):
            for j in range(DRING):
                if uses is not None:
                    sp.wait_ge(downs_used, uses + j)
                sp.dma_start(dring[:, j, :].rearrange("p (c n) -> p c n", c=2),
                             a["w_down"][0, bass.ds(expert, 1), j * 256:(j + 1) * 256, :]
                             .rearrange("e (c p) n -> p (e c) n", p=P)).then_inc(down_in[j], 16)

        expert_up(0, 8, N_MIX - RING + 1)
        expert_up(1, 0, N_MIX - RING + 9)
        sp.wait_ge(pieces_used, N_MIX)
        expert_down(0, None)
        sp.wait_ge(passes_ready, 1)
        more = sp.value_load(more_i32[0:1, 0:1], min_val=0, max_val=PASSES - 1)
        with sp.Fori(0, more * (E // 2) + (E // 2 - 1 - IN_ORDER)) as i:
            expert_up((i * 2 + 2) % E, 8, i * 16 + (N_MIX - RING + 17))
            expert_down((i * 2 + 1) % E, i * 8 + 1)
            expert_up((i * 2 + 3) % E, 0, i * 16 + (N_MIX - RING + 25))
            expert_down((i * 2 + 2) % E, i * 8 + 5)
        ups, downs = more * (KC * E) + (N_MIX - RING + 1), more * (DRING * E) + (1 - DRING)
        e0 = E - 2 * IN_ORDER
        expert_down(e0 - 1, downs + DRING * (e0 - 1))
        with sp.Fori(0, IN_ORDER) as i:
            for u in range(2):
                e = i * 2 + (e0 + u)
                expert_up(e, 8 * (1 - u), ups + e * KC)
                expert_down(e, downs + e * DRING)
        sp.wait_ge(pieces_used, more * (KC * E) + (KC * (E - 1) + N_MIX))
        sp.dma_start(gain_out, a["norm_final_g"].unsqueeze(0).broadcast_to([P, D])).then_inc(final_gain_in, 16)
        for t in range(TT):
            sp.wait_ge(fin_sb, t + 1)
            sp.dma_start(out[0, t * P:(t + 1) * P, :], x2[:, t, :]).then_inc(out_done, 16)
        sp.wait_ge(out_done, 16 * TT)

    @block.gpsimd
    def _(pool):
        pool.wait_ge(dist_sb, 1)
        pool.dma_start(scratch[:, 0:TOEP], bias_of_dist).then_inc(scratch_out, 16)
        pool.wait_ge(scratch_out, 16)
        pool.dma_start(bias, bass.AP(scratch.tensor, 0, [[1, P], [384, ATT_H], [1, 2 * P]])).then_inc(bias_in, 16)
        pool.wait_ge(att_scores_read, ATT_H)
        for q in range(4):
            half = q % 2
            pool.dma_start(b_gu[q * E:(q + 1) * E, :].rearrange("e (k n) -> e k n", k=2),
                           a["b_gu"][0].rearrange("e (k h n) -> e k h n", k=2, h=2)[:, :, half, :])\
                .then_inc(expert_bias_in, 16)
        pool.dma_start(b_down, a["b_down"][0]).then_inc(expert_bias_in, 16)
        pool.wait_ge(merged_sb, 2 * len(GROUPS))
        pool.dma_start(w_rt, a["w_router"][0].rearrange("(c p) e -> p c e", p=P)).then_inc(router_in, 16)
        pool.dma_start(b_rt, a["b_router"].broadcast_to([P, E])).then_inc(router_in, 16)

    @block.scalar
    def _(act):
        act.wait_ge(mean_done, 1)
        act.activation(norm[:, 0, 4:6], norm[:, 0, 2:4], ACT.Sqrt)

        def square_sums(src, into, n, t):
            act.activation(into[:, t, :], src[:, t, :], ACT.Square, accum_out=norm[:, n, t:t + 1]).then_inc(sq_done, 1)

        def root(n):
            act.wait_ge(mean_done, n + 2)
            act.activation(norm[:, n, 4:6], norm[:, n, 2:4], ACT.Sqrt).then_inc(root_done, 1)

        for n, (src, loaded) in enumerate(((x_nat, x_in), (mem_nat, mem_in))):
            for t in range(TT):
                act.wait_ge(loaded[t], 16)
                if n:
                    act.wait_ge(sq_done, TT)
                square_sums(src, squares, n, t)
            root(n)

        def exp(hh):
            act.wait_ge(top_ready, hh + 1)
            pr = probs[hh % 2]
            if hh < ATT_H:
                for n, cut in enumerate((slice(0, 256), slice(256, 384))):
                    last = act.activation(pr[:, cut], pr[:, cut], ACT.Exp, bias=negtop[:, hh, n:n + 1],
                                          accum_out=sums[:, hh, n:n + 1])
            else:
                act.wait_ge(probsT_done, hh - 1)
                for n in range(TT):
                    cut = slice(n * 256, n * 256 + 256)
                    last = act.activation(pr[:, cut], bank[2 + hh % 2][:, cut], ACT.Exp,
                                          bias=negtop[:, hh, n:n + 1], scale=X_D ** -0.5,
                                          accum_out=sums[:, hh, n:n + 1])
            last.then_inc(exp_done, 1)

        def probsT_copy(hh):
            act.wait_ge(probsT_done, hh + 1)
            n = 384 if hh < ATT_H else 512
            act.activation(probsT[hh % 2][:, 0:n], bank[4][:, 0:n], ACT.Copy).then_inc(probsT_sb, 1)

        def pv_copy(hh):
            if hh < ATT_H and hh % 2 == 0:
                return
            u, dst = (hh // 2, qk[:, hh // 2, :]) if hh < ATT_H else (hh - ATT_H // 2, qx[:, hh - ATT_H, :])
            act.wait_ge(pv_done, u + 1)
            act.activation(dst, bank[5][:, (u % 2) * 256:(u % 2) * 256 + 256], ACT.Copy).then_inc(y_att_sb, 1)

        def heads(j, lo, hi):
            if lo <= j < hi:
                exp(j)
            if lo <= j - 2 < hi:
                probsT_copy(j - 2)
            if lo <= j - 3 < hi:
                pv_copy(j - 3)

        for j in range(12):
            heads(j, 0, ATT_H)
        for t in range(4 * len(GROUPS)):
            n = t // 2
            if t % 2 == 0:
                b, _, half = GROUPS[n // 2]
                act.wait_ge(pieces_used, N_PROJ + 3 * (n // 2) + n % 2 + 1)
                if n:
                    act.wait_ge(merged_sb, n)
                for k in range(2):
                    tile = b * 8 + half * 4 + (n % 2) * 2 + k
                    last = act.activation(sig[:, k * 256:k * 256 + 256], bank[n % 2][:, k * 256:k * 256 + 256],
                                          ACT.Sigmoid, bias=b_gate[:, tile:tile + 1])
                last.then_inc(gates_sb, 1)
            else:
                heads(ATT_H + n, ATT_H, HEADS)

        for t in range(TT):
            act.wait_ge(x2_sb, t + 1)
            square_sums(x2, squares2, 2, t)
        root(2)
        act.wait_ge(best_ready, 1)
        for t in range(TT):
            last = act.activation(elog[:, t, :], logit[:, t, :], ACT.Exp, bias=small[:, t:t + 1])
        last.then_inc(router_exp, 1)

        act.wait_ge(passes_ready, 1)
        more = act.value_load(more_i32[0:1, 0:1], min_val=0, max_val=PASSES - 1)
        with act.Fori(0, more * (E // 2) + E // 2) as i:
            for u in range(2):
                s = i * 2 + u
                act.wait_ge(g_ready, s + 1)
                act.activation(sg, g_sb, ACT.Sigmoid, scale=ALPHA).then_inc(sig_ready, 1)
                act.wait_ge(scaT_done, s + 1)
                act.wait_ge(y_ready, s + 1)
                act.activation(unused, y_ps[:, 0:TT * P], ACT.Copy, accum_out=w_slot).then_inc(w_slot_ready, 1)
                act.wait_ge(hidT_done, s + 1)
                act.activation(hidT, tr_ps[:, :], ACT.Copy).then_inc(hidT_sb, 1)
                act.wait_ge(downs_used, (s + 1) * DRING)
                act.wait_ge(w_slot_ready, s + 1)
                act.activation(y_parts[0:64, 0:512], y_ps[0:64, :], ACT.Copy, scale=w_slot[0:64, :])
                act.activation(y_parts[64:128, 512:1024], y_ps[64:128, :], ACT.Copy, scale=w_slot[64:128, :])\
                    .then_inc(y_high, 1)

        for t in range(TT):
            act.wait_ge(sum_ready, t + 1)
            square_sums(x2, h2, 3, t)
            act.wait_ge(mean_done, 5 + t)
            act.activation(norm[:, 3, 4 + t:5 + t], norm[:, 3, 2 + t:3 + t], ACT.Sqrt).then_inc(root_done, 1)

    @block.vector
    def _(dve):
        steps = [0]

        def link(ins):
            steps[0] += 1
            ins.then_inc(dve_step, 1)
            dve.wait_ge(dve_step, steps[0])

        dve.memset(norm[:, 0, 2:4], 1.0).then_inc(mean_done, 1)
        dve.memset(ones[:, :], 1.0)
        dve.memset(z[:, :, 0:2], 0.0)

        def rstd(n):
            dve.wait_ge(sq_done, TT * (n + 1))
            dve.tensor_scalar(norm[:, n, 2:4], norm[:, n, 0:2], 1.0 / D, EPS, ALU.mult, ALU.add).then_inc(mean_done, 1)
            dve.wait_ge(root_done, n + 1)
            link(dve.reciprocal(norm[:, n, 6:8], norm[:, n, 4:6]))

        def normalise(n, src, dst, done):
            for t in range(TT):
                dve.tensor_scalar(dst[:, t, :], src[:, t, :], norm[:, n, 6 + t:7 + t], None, ALU.mult).then_inc(done, 1)

        def with_gain(ps, gain, dst, half, t, done):
            g4 = gain[:, 4 * half:4 * half + 4].unsqueeze(2).broadcast_to([P, 4, P])
            dve.tensor_tensor(dst[:, 4 * half:4 * half + 4, t * P:(t + 1) * P],
                              ps[:, :].rearrange("p (c t) -> p c t", c=4), g4, ALU.mult).then_inc(done, 1)

        dve.wait_ge(dist_done, 1)
        dve.tensor_copy(bias_of_dist, bank[3][0:ATT_H, 0:TOEP]).then_inc(dist_sb, 1)
        dve.wait_ge(cols_done, 1)
        dve.tensor_copy(cols[:, :], bank[2][:, 0:60]).then_inc(cols_sb, 1)
        rstd(0)
        normalise(0, x_nat, x_nat, normed)
        dve.wait_ge(cols_sb, 1)
        for u in range(4):
            dve.wait_ge(hT_done, u + 1)
            with_gain(bank[4 + u], g_mix, hT, u % 2, u // 2, hT_sb)

        def projection(u):
            dve.wait_ge(pieces_used, u + 1)
            ps = bank[u % 2][:, :].rearrange("p (k t) -> p k t", k=2)
            name, col = PROJ[u]
            if name == "w_mem_kv":
                j = col // 256
                ins = (dve.tensor_copy(kx[:, 2 * j:2 * j + 2, :], ps) if j < 2 else
                       dve.tensor_copy(vx[:, :, (j - 2) * 256:(j - 1) * 256], ps))
            elif col < VA:
                ins = dve.tensor_copy(qk[:, col // P:col // P + 2, :], ps)
            elif col < CB:
                ins = dve.tensor_copy(v_att[:, :, col - VA:col - VA + 256], ps)
            elif col >= QX:
                ins = dve.tensor_copy(qx[:, (col - QX) // P:(col - QX) // P + 2, :], ps)
            elif col >= CU:
                k = (col - CU) // P
                dve.wait_ge(proj_sb, u - 1)
                ins = dve.tensor_tensor(z[:, k:k + 2, 2:], ps, z[:, k:k + 2, 2:], ALU.mult)
            elif col >= CC:
                k = (col - CC) // P
                ins = dve.tensor_copy(z[:, k:k + 2, 2:], ps)
            else:
                k = (col - CB) // P
                ins = dve.tensor_tensor(y_conv[:, k:k + 2, :], ps, y_conv[:, k:k + 2, :], ALU.mult)
            ins.then_inc(proj_sb, 1)
            if name == "w_in" and CU <= col < QX:
                dve.wait_ge(proj_sb, u + 1)
                for c in range(k, k + 2):
                    link(dve.tensor_scalar(y_conv[:, c, :], z[:, c, 0:S], conv_w[:, c:c + 1], None, ALU.mult))
                    for tap in (1, 2):
                        w = conv_w[:, 4 * tap + c:4 * tap + c + 1]
                        link(dve.scalar_tensor_tensor(y_conv[:, c, :], z[:, c, tap:tap + S], w, y_conv[:, c, :],
                                                      ALU.mult, ALU.add))

        def head_top(hh):
            dve.wait_ge(scores_done, hh + 1)
            ps, pr = bank[2 + hh % 2], probs[hh % 2]
            if hh < ATT_H:
                if hh == 0:
                    dve.wait_ge(bias_sb, 4)
                if hh >= 2:
                    dve.wait_ge(probsT_done, hh - 1)
                dve.scalar_tensor_tensor(pr[:, 0:256], ps[:, 0:256], ATT_D ** -0.5, bias[:, hh, :], ALU.mult, ALU.add)
                dve.scalar_tensor_tensor(pr[:, 256:384], ps[:, 256:384], ATT_D ** -0.5, bias[:, hh, 128:256],
                                         ALU.mult, ALU.add).then_inc(att_scores_read, 1)
                dve.wait_ge(att_scores_read, hh + 1)
                dve.tensor_reduce(top[:, hh, 0:1], pr[:, 0:256], AX.X, ALU.max)
                link(dve.tensor_reduce(top[:, hh, 1:2], pr[:, 256:384], AX.X, ALU.max))
                scale = 1.0
            else:
                link(dve.tensor_reduce(top[:, hh, :], ps[:, :].rearrange("p (t k) -> p t k", t=TT), AX.X, ALU.max))
                scale = X_D ** -0.5
            dve.tensor_scalar(negtop[:, hh, :], top[:, hh, :], -scale, None, ALU.mult).then_inc(top_ready, 1)

        def head_norm(hh):
            dve.wait_ge(exp_done, hh + 1)
            link(dve.reciprocal(top[:, hh, :], sums[:, hh, :]))
            pr = probs[hh % 2]
            cuts = (slice(0, 256), slice(256, 384 if hh < ATT_H else 512))
            for n, cut in enumerate(cuts):
                last = dve.tensor_scalar(pr[:, cut], pr[:, cut], top[:, hh, n:n + 1], None, ALU.mult)
            last.then_inc(probs_ready, 1)

        def heads(j, lo, hi):
            if lo <= j < hi:
                head_top(j)
            if lo <= j - 1 < hi:
                head_norm(j - 1)

        for u in range(4):
            projection(u)
        for j in range(4):
            dve.wait_ge(bias_flipped, j + 1)
            dve.tensor_copy(bias[:, 2 * j:2 * j + 2, :], bank[2 + j % 2][:, :].rearrange("p (h k) -> p h k", h=2))\
                .then_inc(bias_sb, 1)
        rstd(1)
        normalise(1, mem_nat, mem_nat, normed)
        for u in range(4):
            dve.wait_ge(hT_done, 4 + u + 1)
            with_gain(bank[4 + u], g_mem, memT, u % 2, u // 2, hT_sb)
        projection(4)
        projection(5)
        for j in range(12):
            projection(6 + j)
            heads(j, 0, ATT_H)

        for n in range(2 * len(GROUPS)):
            heads(ATT_H + n, ATT_H, HEADS)
            g = n // 2
            tile = GROUPS[g][2] * 4 + (n % 2) * 2
            dst = merged[:, tile:tile + 2, :].rearrange("p c t -> p (c t)")
            dve.wait_ge(gates_sb, n + 1)
            if n % 2:
                dve.wait_ge(pieces_used, N_PROJ + 3 * g + 3)
            else:
                dve.wait_ge(branch_done, g + 1)
            if g < 2:
                dve.tensor_tensor(dst, bank[6 + n % 2][:, :], sig, ALU.mult).then_inc(merged_sb, 1)
            else:
                link(dve.tensor_tensor(prod, bank[6 + n % 2][:, :], sig, ALU.mult))
                dve.wait_ge(merged_sb, n)
                dve.tensor_tensor(dst, dst, prod, ALU.add).then_inc(merged_sb, 1)

        dve.wait_ge(x_again_in, 16)
        dve.wait_ge(pieces_used, N_MIX)
        for t in range(TT):
            for half in range(2):
                cut = slice(half * 512, half * 512 + 512)
                last = dve.tensor_tensor(x2[:, t, cut], bank[2 + 2 * t + half][:, :], x_again[:, t, cut], ALU.add)
            last.then_inc(x2_sb, 1)
        rstd(2)
        dve.wait_ge(x2_sb, TT)
        normalise(2, x2, h2, h2_sb)
        for u in range(4):
            dve.wait_ge(h2T_done, u + 1)
            with_gain(bank[(6, 7, 0, 1)[u]], g_ffn, h2T, u % 2, u // 2, h2T_sb)

        dve.wait_ge(router_in, 32)
        dve.wait_ge(logits_done, 1)
        link(dve.tensor_tensor(logit, bank[4][:, 0:TT * E].rearrange("p (t e) -> p t e", t=TT),
                               b_rt.unsqueeze(1).broadcast_to([P, TT, E]), ALU.add))
        dve.max(best[:, 0, :], logit[:, 0, :])
        link(dve.max(best[:, 1, :], logit[:, 1, :]))
        dve.tensor_scalar(small[:, 0:2], best[:, :, 0], -1.0, None, ALU.mult).then_inc(best_ready, 1)
        dve.max_index(best_u[:, 0, :], best[:, 0, :], logit[:, 0, :])
        link(dve.max_index(best_u[:, 1, :], best[:, 1, :], logit[:, 1, :]))
        link(dve.tensor_copy(best_i, best_u[:, :, :]))
        for k in range(TOPK):
            for t in range(TT):
                if k == 0:
                    last = dve.tensor_scalar(mask[:, t, :], slot_no[:, 0:E], best_i[:, t, 0:1], None, ALU.is_equal)
                else:
                    last = dve.scalar_tensor_tensor(mask[:, t, :], slot_no[:, 0:E], best_i[:, t, k:k + 1],
                                                    mask[:, t, :], ALU.is_equal, ALU.add)
            if k < TOPK - 1:
                link(last)
        last.then_inc(mask_sb, 1)

        dve.wait_ge(router_exp, 1)
        dve.wait_ge(mask_sb, 1)
        link(dve.tensor_tensor(elog, elog, mask, ALU.mult))
        link(dve.tensor_reduce(small[:, 2:4], elog, AX.X, ALU.add))
        link(dve.reciprocal(small[:, 4:6], small[:, 2:4]))
        for t in range(TT):
            for b in range(PASSES):
                last = dve.tensor_scalar(wexp[:, t, b * E:(b + 1) * E], elog[:, t, :], small[:, 4 + t:5 + t], None, ALU.mult)
        dve.memset(wexp[:, :, STEPS:], 0.0)
        last = dve.memset(place[:, :, STEPS:], -1.0)
        last.then_inc(weights_sb, 1)

        dve.wait_ge(rank_done, 1)
        link(dve.scalar_tensor_tensor(rank, bank[5][:, 0:TT * E].rearrange("p (t e) -> p t e", t=TT), 1.0, mask,
                                      ALU.add, ALU.mult))
        for b in range(PASSES):
            dve.tensor_scalar(place[:, :, b * E:(b + 1) * E], rank, -1.0 - SLOTS * b, None, ALU.add)
        link(dve.tensor_reduce(small[:, 6:7], bank[5][:, TT * E:(TT + 1) * E], AX.X, ALU.max))
        link(dve.tensor_scalar(small[:, 7:8], small[:, 6:7], float(SLOTS), None, ALU.is_gt))
        for b in range(2, PASSES):
            link(dve.scalar_tensor_tensor(small[:, 6 + b:7 + b], small[:, 6:7], float(SLOTS * b),
                                          small[:, 5 + b:6 + b], ALU.is_gt, ALU.add))
        dve.tensor_copy(more_i32[0:1, 0:1], small[0:1, 5 + PASSES:6 + PASSES]).then_inc(passes_ready, 1)
        dve.wait_ge(wexpT_done, 1)
        dve.tensor_copy(wexpT, bank[6][0:E, 0:TT * P]).then_inc(wexpT_sb, 1)

        def gather_matrix(s):
            for t in range(TT):
                last = dve.tensor_scalar(gat[:, t, :], slot_no[:, 0:SLOTS], place[:, t, bass.ds(s, 1)], None, ALU.is_equal)
            last.then_inc(gat_ready, 1)

        def scatter_matrix(s):
            for t in range(TT):
                last = dve.tensor_scalar(sca[:, t, :], slot_no, place[:, t, bass.ds(s, 1)], wexp[:, t, bass.ds(s, 1)],
                                         ALU.is_equal, ALU.mult)
            last.then_inc(sca_ready, 1)

        def bias_selector(s):
            dve.tensor_scalar(sel[:, :], half_of, pick[:, bass.ds(s, 1)], None, ALU.mult).then_inc(sel_ready, 1)

        gather_matrix(0)
        scatter_matrix(0)
        bias_selector(0)
        dve.wait_ge(acc_open, 1)
        dve.wait_ge(expert_bias_in, 16 * 5)
        dve.tensor_copy(b_parts[0:64, :], b_gu[0:64, :])
        link(dve.tensor_copy(y_parts[64:128, :], b_gu[64:128, :]))
        dve.tensor_tensor(b_parts[64:128, :], b_gu[64:128, :], y_parts[64:128, :].bitcast(fp32), ALU.subtract)\
            .then_inc(b_parts_ready, 1)
        dve.wait_ge(b_parts_ready, 1)
        link(dve.memset(zero[:, :], 0.0))
        dve.tensor_copy(scaT[:, :, :].rearrange("p t s -> p (t s)"), zero[:, 0:1].broadcast_to([P, TT * P])).then_inc(scaT_sb, 1)
        dve.tensor_copy(y_parts[:, :], zero[:, 0:1].broadcast_to([P, 1024])).then_inc(y_ready, 1)
        dve.memset(hidT[:, 0:2], 0.0).then_inc(hidT_sb, 1)
        dve.memset(g_sb[:, 0:2], 0.0).then_inc(up_read, 1)
        dve.wait_ge(gathered, 1)
        dve.tensor_tensor(xg, tr_ps[:, :].rearrange("p (c s) -> p c s", c=KC),
                          g_ffn.unsqueeze(2).broadcast_to([P, KC, SLOTS]), ALU.mult).then_inc(xg_sb, 1)

        more = dve.value_load(more_i32[0:1, 0:1], min_val=0, max_val=PASSES - 1)
        with dve.Fori(0, more * (E // 2) + E // 2) as i:
            for u in range(2):
                s = i * 2 + u
                dve.wait_ge(gathered, s + 1)
                gather_matrix(s + 1)
                dve.wait_ge(pieces_used, (s + 1) * KC + N_MIX)
                dve.tensor_scalar(g_sb, gate_ps[:, :], LIMIT, None, ALU.min).then_inc(g_ready, 1)
                dve.tensor_scalar(hid, lin_ps[:, :], LIMIT, -LIMIT, ALU.min, ALU.max).then_inc(up_read, 1)
                dve.wait_ge(g_ready, s + 1)
                dve.wait_ge(up_read, s + 2)
                dve.scalar_tensor_tensor(hid, hid, 1.0, g_sb, ALU.add, ALU.mult).then_inc(hid_half, 1)
                dve.wait_ge(hid_half, s + 1)
                dve.wait_ge(sig_ready, s + 1)
                dve.tensor_tensor(hid, hid, sg, ALU.mult).then_inc(hid_ready, 1)
                dve.wait_ge(w_slot_ready, s + 1)
                dve.wait_ge(scattered, s + 1)
                dve.tensor_scalar(scaT[:, :, :].rearrange("p t s -> p (t s)"), y_ps[:, 0:TT * P], 0.0, None, ALU.not_equal)\
                    .then_inc(scaT_sb, 1)
                bias_selector(s + 1)
                dve.wait_ge(gathered, s + 2)
                dve.tensor_tensor(xg, tr_ps[:, :].rearrange("p (c s) -> p c s", c=KC),
                                  g_ffn.unsqueeze(2).broadcast_to([P, KC, SLOTS]), ALU.mult).then_inc(xg_sb, 1)
                scatter_matrix(s + 1)
                dve.wait_ge(downs_used, (s + 1) * DRING)
                dve.wait_ge(y_high, s + 1)
                dve.scalar_tensor_tensor(y_parts[64:128, 0:512], y_ps[0:64, :], w_slot[0:64, :],
                                         y_parts[0:64, 0:512].bitcast(fp32), ALU.mult, ALU.subtract)
                dve.scalar_tensor_tensor(y_parts[0:64, 512:1024], y_ps[64:128, :], w_slot[64:128, :],
                                         y_parts[64:128, 512:1024].bitcast(fp32), ALU.mult, ALU.subtract)\
                    .then_inc(y_ready, 1)

        dve.wait_ge(acc_done, 1)
        dve.wait_ge(final_gain_in, 16)
        for t in range(TT):
            for half in range(2):
                cut = slice(half * 512, half * 512 + 512)
                last = dve.tensor_tensor(x2[:, t, cut], acc[t][half][:, :], x2[:, t, cut], ALU.add)
            last.then_inc(sum_ready, 1)
        for t in range(TT):
            dve.wait_ge(sq_done, 3 * TT + t + 1)
            dve.tensor_scalar(norm[:, 3, 2 + t:3 + t], norm[:, 3, t:t + 1], 1.0 / D, EPS, ALU.mult, ALU.add)\
                .then_inc(mean_done, 1)
            dve.wait_ge(root_done, 4 + t)
            link(dve.reciprocal(norm[:, 3, 6 + t:7 + t], norm[:, 3, 4 + t:5 + t]))
            dve.scalar_tensor_tensor(x2[:, t, :], x2[:, t, :], norm[:, 3, 6 + t:7 + t], gain_out, ALU.mult, ALU.mult)\
                .then_inc(fin_sb, 1)

    @block.tensor
    def _(pe):
        mm, transpose = pe.matmul, pe.transpose

        def loaded(p):
            pe.wait_ge(piece_in[p % RING], 16 * (p // RING + 1))
            return ring[:, p % RING, :]

        def transposed(src, u, out_bank, done):
            t, half = u // 2, u % 2
            for c in range(4):
                last = transpose(out_bank[:, c * P:(c + 1) * P], src[:, t, (4 * half + c) * P:(4 * half + c + 1) * P], ident)
            last.then_inc(done, 1)

        pe.wait_ge(table_in, 16)
        mm(bank[3][0:ATT_H, 0:TOEP], table, hot, start=True, stop=True).then_inc(dist_done, 1)
        pe.wait_ge(rows_in, 16 * 3)
        transpose(bank[2][:, 0:60], rows, ident[0:60, 0:60]).then_inc(cols_done, 1)
        for u in range(4):
            pe.wait_ge(normed, u // 2 + 1)
            transposed(x_nat, u, bank[4 + u], hT_done)

        def projection(u):
            if u >= 2:
                pe.wait_ge(proj_sb, u - 1)
            w = loaded(u).rearrange("p (c n) -> p c n", c=KC)
            name, col = PROJ[u]
            src = hT if name == "w_in" else memT
            values = VA <= col < CB if name == "w_in" else col >= 512
            for k in range(2):
                dst, cut = bank[u % 2][:, k * 256:k * 256 + 256], slice(k * P, k * P + P)
                for c in range(KC):
                    lhsT, rhs = (src[:, c, cut], w[:, c, :]) if values else (w[:, c, cut], src[:, c, :])
                    last = mm(dst, lhsT, rhs, start=(c == 0), stop=(c == KC - 1))
            last.then_inc(pieces_used, 1)

        def scores(hh):
            dst = bank[2 + hh % 2]
            if hh < ATT_H:
                if hh >= 2:
                    pe.wait_ge(att_scores_read, hh - 1)
                else:
                    pe.wait_ge(bias_sb, 3 + hh)
                q = qk[64 * (hh % 2):64 * (hh % 2) + 64, hh // 2, :]
                k = qk[64 * (hh % 2):64 * (hh % 2) + 64, 4 + hh // 2, :]
                mm(dst[:, 0:256], q[:, P:2 * P], k, start=True, stop=True)
                mm(dst[:, 256:384], q[:, 0:P], k[:, 0:P], start=True, stop=True).then_inc(scores_done, 1)
            else:
                if hh < ATT_H + 2:
                    pe.wait_ge(att_scores_read, hh - 1)
                else:
                    pe.wait_ge(exp_done, hh - 1)
                for t in range(TT):
                    last = mm(dst[:, t * 256:t * 256 + 256], qx[:, hh - ATT_H, t * P:(t + 1) * P], kx[:, hh - ATT_H, :],
                              start=True, stop=True)
                last.then_inc(scores_done, 1)

        def probs_transposed(hh):
            pe.wait_ge(probs_ready, hh + 1)
            if hh:
                pe.wait_ge(probsT_sb, hh)
            pr, dst = probs[hh % 2], bank[4]
            moves = ([(0, 256), (128, 0), (256, 128)] if hh < ATT_H else
                     [(k * 256 + t * P, t * 256 + k * P) for k in range(2) for t in range(TT)])
            for to, at in moves:
                last = transpose(dst[:, to:to + P], pr[:, at:at + P], ident)
            last.then_inc(probsT_done, 1)

        def values(hh):
            pe.wait_ge(probsT_sb, hh + 1)
            pT = probsT[hh % 2]
            u = hh // 2 if hh < ATT_H else hh - ATT_H // 2
            if u:
                pe.wait_ge(y_att_sb, u)
            if hh < ATT_H:
                dst = bank[5][64 * (hh % 2):64 * (hh % 2) + 64, (u % 2) * 256:(u % 2) * 256 + 256]
                mm(dst, v_att[:, 0, 64 * hh:64 * hh + 64], pT[:, 0:256], start=True, stop=False)
                last = mm(dst[:, P:2 * P], v_att[:, 1, 64 * hh:64 * hh + 64], pT[:, 256:384], start=False, stop=True)
                if hh % 2:
                    last.then_inc(pv_done, 1)
            else:
                x = hh - ATT_H
                dst = bank[5][:, (u % 2) * 256:(u % 2) * 256 + 256]
                for k in range(2):
                    last = mm(dst, vx[:, k, x * P:(x + 1) * P], pT[:, k * 256:k * 256 + 256], start=(k == 0), stop=(k == 1))
                last.then_inc(pv_done, 1)

        def heads(j, lo, hi):
            if lo <= j < hi:
                scores(j)
            if lo <= j - 2 < hi:
                probs_transposed(j - 2)
            if lo <= j - 3 < hi:
                values(j - 3)

        pe.wait_ge(hT_sb, 4)
        for u in range(4):
            projection(u)
        pe.wait_ge(bias_in, 16)
        pe.wait_ge(cols_sb, 1)
        pe.wait_ge(dist_sb, 1)
        for j in range(4):
            if j >= 2:
                pe.wait_ge(bias_sb, j - 1)
            mm(bank[2 + j % 2][:, :], flip, bias[:, 2 * j:2 * j + 2, :].rearrange("p h k -> p (h k)"),
               start=True, stop=True).then_inc(bias_flipped, 1)
        for u in range(4):
            pe.wait_ge(normed, TT + u // 2 + 1)
            transposed(mem_nat, u, bank[4 + u], hT_done)
        projection(4)
        projection(5)
        pe.wait_ge(hT_sb, 8)
        for j in range(12):
            projection(6 + j)
            heads(j, 0, ATT_H)

        def gate_logits(n):
            g = n // 2
            w = loaded(N_PROJ + 3 * g + n % 2).rearrange("p (c n) -> p c n", c=KC)
            if n < 2:
                pe.wait_ge(proj_sb, N_PROJ - 1 + n)
            else:
                pe.wait_ge(gates_sb, n - 1)
            for k in range(2):
                for c in range(KC):
                    last = mm(bank[n % 2][:, k * 256:k * 256 + 256], w[:, c, k * P:(k + 1) * P], hT[:, c, :],
                              start=(c == 0), stop=(c == KC - 1))
            last.then_inc(pieces_used, 1)

        def branch(g, second):
            b = GROUPS[g][0]
            w = loaded(N_PROJ + 3 * g + 2).rearrange("p (c n) -> p c n", c=4)
            y = {1: y_conv, 0: qk, 2: qx}[b]
            if b != 1:
                pe.wait_ge(y_att_sb, ATT_H // 2 + (X_H if b == 2 else 0))
            if g:
                pe.wait_ge(merged_sb, 2 * g - 1 + second)
            for k in range(2):
                at = (2 * second + k) * P
                for c in range(4):
                    last = mm(bank[6 + second][:, k * 256:k * 256 + 256], w[:, c, at:at + P], y[:, c, :],
                              start=(c == 0), stop=(c == 3))
            last.then_inc(pieces_used if second else branch_done, 1)

        for n in range(2 * len(GROUPS)):
            gate_logits(n)
            branch(n // 2, n % 2)
            heads(ATT_H + n, ATT_H, HEADS)

        pe.wait_ge(exp_done, HEADS)
        pe.wait_ge(probsT_sb, HEADS)
        pe.wait_ge(y_att_sb, ATT_H // 2 + X_H)
        for j in range(4):
            pe.wait_ge(merged_sb, 10 if j < 2 else 12)
            w = loaded(N_MIX - 4 + j).rearrange("p (c n) -> p c n", c=2)
            for k in range(2):
                c = 2 * j + k
                for t in range(TT):
                    for half in range(2):
                        last = mm(bank[2 + 2 * t + half][:, :], merged[:, c, t * P:(t + 1) * P],
                                  w[:, k, half * 512:half * 512 + 512], start=(c == 0), stop=(c == KC - 1))
            last.then_inc(pieces_used, 1)

        pe.wait_ge(merged_sb, 12)
        pe.wait_ge(gates_sb, 12)
        for u in range(4):
            pe.wait_ge(h2_sb, u // 2 + 1)
            transposed(h2, u, bank[(6, 7, 0, 1)[u]], h2T_done)
        pe.wait_ge(h2T_sb, 4)
        pe.wait_ge(router_in, 32)
        pe.wait_ge(x2_sb, TT)
        for t in range(TT):
            for c in range(KC):
                last = mm(bank[4][:, t * E:(t + 1) * E], h2T[:, c, t * P:(t + 1) * P], w_rt[:, c, :],
                          start=(c == 0), stop=(c == KC - 1))
        last.then_inc(logits_done, 1)
        pe.wait_ge(mask_sb, 1)
        mm(bank[5][:, 0:E], before, mask[:, 0, :], start=True, stop=True)
        mm(bank[5][:, E:2 * E], ones[:, :], mask[:, 0, :], start=True, stop=False)
        mm(bank[5][:, E:2 * E], before, mask[:, 1, :], start=False, stop=True)
        mm(bank[5][:, 2 * E:3 * E], ones[:, :], mask[:, 0, :], start=True, stop=False)
        mm(bank[5][:, 2 * E:3 * E], ones[:, :], mask[:, 1, :], start=False, stop=True).then_inc(rank_done, 1)
        pe.wait_ge(weights_sb, 1)
        for t in range(TT):
            last = mm(bank[6][0:E, t * P:(t + 1) * P], wexp[:, t, 0:E], ident, start=True, stop=True)
        last.then_inc(wexpT_done, 1)
        pe.wait_ge(wexpT_sb, 1)
        pe.wait_ge(expert_bias_in, 16 * 5)
        for t in range(TT):
            for half in range(2):
                last = mm(acc[t][half][:, :], wexpT[:, t * P:(t + 1) * P], b_down[:, half * 512:half * 512 + 512],
                          start=True, stop=False)
        last.then_inc(acc_open, 1)

        def gather(s):
            pe.wait_ge(gat_ready, s + 1)
            for c in range(KC):
                for t in range(TT):
                    last = mm(tr_ps[:, c * SLOTS:(c + 1) * SLOTS], h2[:, t, c * P:(c + 1) * P], gat[:, t, :],
                              start=(t == 0), stop=(t == TT - 1))
            last.then_inc(gathered, 1)

        def scatter(stop):
            for t in range(TT):
                for half in range(2):
                    last = mm(acc[t][half][:, :], scaT[:, t, :], y_parts[:, half * 512:half * 512 + 512],
                              start=False, stop=stop)
            return last

        gather(0)
        pe.wait_ge(b_parts_ready, 1)
        more = pe.value_load(more_i32[0:1, 0:1], min_val=0, max_val=PASSES - 1)
        with pe.Fori(0, more * (E // 2) + E // 2) as i:
            for u in range(2):
                s = i * 2 + u
                slot0 = 8 if u == 0 else 0
                uses = i * 16 + 16 * ((N_MIX + 8 * u) // RING + 1)
                pe.wait_ge(sel_ready, s + 1)
                pe.wait_ge(up_read, s + 1)
                for k, ps in enumerate((gate_ps, lin_ps)):
                    mm(ps[:, :], sel[:, :], b_parts[:, k * 512:k * 512 + 512], start=True, stop=False)
                pe.wait_ge(xg_sb, s + 1)
                for c in range(KC):
                    pe.wait_ge(piece_in[slot0 + c], uses)
                    for k, ps in enumerate((gate_ps, lin_ps)):
                        for half in range(2):
                            last = mm(ps[64 * half:64 * half + 64, :], xg[:, c, :],
                                      ring[:, slot0 + c, k * F + half * 512:k * F + half * 512 + 512],
                                      start=False, stop=(c == KC - 1))
                    last.then_inc(pieces_used, 1)
                pe.wait_ge(y_ready, s + 1)
                pe.wait_ge(scaT_sb, s + 1)
                scatter(False).then_inc(scattered, 1)
                pe.wait_ge(sca_ready, s + 1)
                for t in range(TT):
                    last = transpose(y_ps[:, t * P:(t + 1) * P], sca[:, t, :], ident)
                last.then_inc(scaT_done, 1)
                pe.wait_ge(hidT_sb, s + 1)
                gather(s + 1)
                pe.wait_ge(hid_ready, s + 1)
                pe.wait_ge(xg_sb, s + 2)
                for c in range(4):
                    last = transpose(tr_ps[:, c * P:(c + 1) * P], hid[:, c * P:(c + 1) * P], ident)
                last.then_inc(hidT_done, 1)
                pe.wait_ge(hidT_sb, s + 2)
                pe.wait_ge(scaT_sb, s + 2)
                pe.wait_ge(w_slot_ready, s + 1)
                for c in range(KC):
                    if c % 2 == 0:
                        pe.wait_ge(down_in[c // 2], (s + 1) * 16)
                    lhsT = hidT[:, (c % 4) * P + 64 * (c // 4):(c % 4) * P + 64 * (c // 4) + 64]
                    for half in range(2):
                        at = (c % 2) * D + half * 512
                        last = mm(y_ps[64 * half:64 * half + 64, :], lhsT, dring[:, c // 2, at:at + 512],
                                  start=(c == 0), stop=(c == KC - 1))
                    if c % 2:
                        last.then_inc(downs_used, 1)
        pe.wait_ge(y_ready, more * E + (E + 1))
        pe.wait_ge(scaT_sb, more * E + (E + 1))
        scatter(True).then_inc(acc_done, 1)



_INS = ["x", "mem", "rel_bias", "norm_mix_g", "w_in", "b_gate", "conv_w", "norm_mem_g", "w_mem_kv",
        "w_br_att", "w_br_conv", "w_br_xatt", "w_out", "norm_ffn_g", "w_router", "b_router",
        "w_gu", "b_gu", "w_down", "b_down", "norm_final_g"]


def kernel(**inputs):
    import numpy as _np
    import concourse.bacc as _bacc
    from concourse import mybir as _mybir
    from concourse.bass_utils import run_bass_kernel_spmd as _run

    nc = _bacc.Bacc("TRN2", target_bir_lowering=False, num_devices=1)
    given = {name: _np.ascontiguousarray(inputs[name]) for name in _INS}
    given["consts"], hot = shape_constants()
    given["rows"] = _np.concatenate([given.pop(k).reshape(-1, P) for k in
                                     ("norm_mix_g", "norm_mem_g", "norm_ffn_g", "b_gate", "conv_w")])
    future = _np.full((1, ATT_H), NEG, _np.float32)
    given["table_hot"] = _np.concatenate([_np.concatenate([given.pop("rel_bias"), future]), hot], axis=1)
    arrays, args = {}, {}
    for name, value in given.items():
        arrays[f"in_{name}_dram"] = value
        args[name] = nc.dram_tensor(f"in_{name}_dram", value.shape, _mybir.dt.from_np(value.dtype), kind="ExternalInput").ap()
    out = nc.dram_tensor("out_0_dram", (1, S, D), _mybir.dt.float32, kind="ExternalOutput").ap()
    scratch = nc.dram_tensor("bias_scratch", [ATT_H, 384], _mybir.dt.float32, kind="Internal").ap()
    trunk_layer(nc, args, out, scratch)
    r = _run(nc, [arrays], core_ids=[0])
    return r.results[0]["out_0_dram"]
```

```python
import concourse.bass as bass
from concourse import mybir
import numpy as np
import math
from contextlib import ExitStack

P = 128
D = 1024
S = 256
M = 256
ATT_H, ATT_D = 8, 64
X_H, X_D = 4, 128
CONV = 512
E = 32
TOPK = 4
BUCKETS = 32
MAX_DIST = 128
EPS = 1e-5
NEG = -1e30
LIMIT = 7.0
ALPHA = 1.702
F = D
KC = D // P
TT = S // P
SLOTS = 64
PASSES = S // SLOTS
STEPS = PASSES * E
TOEP = 3 * P - 1
RING = 16
PIECE = 2048
DRING = 4
IN_ORDER = 4

QA, KA, VA, CB, CC, CU, QX, GL = 0, 512, 1024, 1536, 2048, 2560, 3072, 3584
PROJ = ([("w_mem_kv", 256 * j) for j in range(4)]
        + [("w_in", col + 256 * j) for col in (QA, KA, VA, CC, CU, CB, QX) for j in range(2)])
BRANCHES = [(1, "w_br_conv"), (0, "w_br_att"), (2, "w_br_xatt")]
GROUPS = [(b, w, half) for b, w in BRANCHES for half in range(2)]
N_PROJ = len(PROJ)
FIRST_HEAD = N_PROJ - ATT_H
N_MIX = N_PROJ + 3 * len(GROUPS) + 4
HEADS = ATT_H + X_H
MIX_RING = 12


def merged_tile(n):
    return GROUPS[n // 2][2] * 4 + (n % 2) * 2


def mixer_slot(p):
    return (p + 8 - (N_MIX - MIX_RING)) % MIX_RING


def mixer_loads(p):
    return sum(mixer_slot(q) == mixer_slot(p) for q in range(p + 1))


def loads_before(slot):
    return sum(mixer_slot(q) == slot for q in range(N_MIX))


C_ID, C_TRI, C_SLOT, C_HALF, C_PICK = 0, P, 2 * P, 3 * P, 4 * P
C_KEPT = C_PICK + STEPS + 1


def shape_constants():
    c = np.zeros((P, C_KEPT + P), np.float32)
    r = np.arange(P)
    c[:, C_ID:C_ID + P] = np.eye(P)
    c[:, C_TRI:C_TRI + P] = np.triu(np.ones((P, P)), 1)
    c[:, C_SLOT:C_SLOT + P] = np.tile(np.arange(SLOTS), 2)[None]
    c[:, C_HALF:C_HALF + P] = (r[:, None] % (2 * E) // E) == (r[None] // SLOTS)
    c[:, C_PICK:C_KEPT] = (r[:, None] % E) == (np.arange(STEPS + 1)[None] % E)
    c[:, C_KEPT:] = np.eye(P)[::-1]
    hot = np.zeros((BUCKETS + 1, TOEP), np.float32)
    exact = BUCKETS // 2
    for i in range(TOEP):
        dist = 2 * P - 1 - i
        if dist < 0:
            hot[BUCKETS, i] = 1.0
        elif dist < exact:
            hot[dist, i] = 1.0
        else:
            large = exact + int(math.log(dist / exact) / math.log(MAX_DIST / exact) * (BUCKETS - exact))
            hot[min(large, BUCKETS - 1), i] = 1.0
    return c, hot


def trunk_layer(nc, a, out, scratch):
    ctx = ExitStack()
    with ctx:
        build(nc, a, out, scratch, ctx)


def build(nc, a, out, scratch, ctx):
    fp32 = mybir.dt.float32
    fp32r = mybir.dt.float32r
    i32 = mybir.dt.int32
    u32 = mybir.dt.uint32
    ALU = mybir.AluOpType
    ACT = mybir.ActivationFunctionType
    AX = mybir.AxisListType

    def sb(name, shape, dt=fp32):
        return nc.alloc_sbuf_tensor(name, shape, dt)

    at_of = {}

    def region(name, shape):
        tensor = sb(name, shape)
        at_of[name] = nc.sbuf_base - 4 * math.prod(shape[1:])
        return tensor

    def rounded(name, shape, where, at):
        return nc.alloc_sbuf_tensor_at(name, shape, fp32r, offset=at_of[where] + 4 * at)

    ring = region("ring", [P, RING, PIECE])
    dring = region("dring", [P, DRING, PIECE])
    region_x = region("region_x", [P, 2048])
    region_h = region("region_h", [P, 2048])
    region_r = region("region_r", [P, 6152])

    scaT = rounded("scaT", [P, TT, P], "region_r", 5000)
    sel = rounded("sel", [P, P], "region_r", 5256)
    b_parts = rounded("b_parts", [P, 1024], "region_r", 0)
    y_parts = sb("y_parts", [P, 1024], fp32r)
    consts = sb("consts", [P, C_KEPT])
    ones = sb("ones", [P, P])
    cols = sb("cols", [P, 60])
    zero = sb("zero", [P, 2])
    stats = sb("stats", [P, 3, HEADS, 2])
    norm = sb("norm", [P, 4, 8])
    more_i32 = sb("more_i32", [1, 1], i32)
    best_u = sb("best_u", [P, TT, 8], u32)

    ident = consts[:, C_ID:C_ID + P]
    before = consts[:, C_TRI:C_TRI + P]
    slot_no = consts[:, C_SLOT:C_SLOT + P]
    half_of = consts[:, C_HALF:C_HALF + P]
    pick = consts[:, C_PICK:C_KEPT]
    g_mix, g_mem, g_ffn = cols[:, 0:8], cols[:, 8:16], cols[:, 16:24]
    b_gate = cols[:, 24:48]
    conv_w = cols[:, 48:60]
    top, negtop, sums = stats[:, 0], stats[:, 1], stats[:, 2]

    w_high = [rounded(f"w_high{n}", [P, PIECE], "ring", (13 + n) * PIECE) for n in range(3)]
    w_low = [rounded(f"w_low{n}", [P, PIECE], "ring", n * PIECE) for n in range(MIX_RING)]
    hT = dring[:, 0, :].rearrange("p (c t) -> p c t", c=KC)
    hT_low = rounded("hT_low", [P, KC, S], "dring", 0)
    hT_high = rounded("hT_high", [P, KC, S], "dring", PIECE)
    memT = dring[:, 2, :].rearrange("p (c t) -> p c t", c=KC)
    memT_low = rounded("memT_low", [P, KC, M], "dring", 2 * PIECE)
    memT_high = rounded("memT_high", [P, KC, M], "dring", 3 * PIECE)
    qk = dring[:, 2, :].rearrange("p (c t) -> p c t", c=8)
    y_att_high = rounded("y_att_high", [P, 4, S], "dring", 2 * PIECE)
    y_att_low = rounded("y_att_low", [P, 4, S], "dring", 2 * PIECE + 1024)
    merged = dring[:, 3, :].rearrange("p (c t) -> p c t", c=KC)
    merged_low = rounded("merged_low", [P, KC, S], "dring", 3 * PIECE)
    merged_high = rounded("merged_high", [P, KC, S], "region_r", 0)
    mem_nat = region_x[:, :].rearrange("p (t d) -> p t d", t=TT)
    qx = region_x[:, 0:1024].rearrange("p (c t) -> p c t", c=X_H)
    kx = region_x[:, 1024:2048].rearrange("p (c t) -> p c t", c=X_H)
    y_x_high = rounded("y_x_high", [P, X_H, S], "region_x", 0)
    y_x_low = rounded("y_x_low", [P, X_H, S], "region_x", 1024)
    x2 = mem_nat
    x_nat = region_h[:, :].rearrange("p (t d) -> p t d", t=TT)
    probs = [region_h[:, 512 * n:512 * n + 512] for n in range(2)]
    probsT = [region_h[:, 1024 + 512 * n:1024 + 512 * n + 512] for n in range(2)]
    x_again = x_nat
    h2 = x_nat
    squares = ring[:, 13, :].rearrange("p (t d) -> p t d", t=TT)
    bias = region_r[:, 0:2048].rearrange("p (h k) -> p h k", h=ATT_H)
    v_att = region_r[:, 2048:3072].rearrange("p (t c) -> p t c", t=TT)
    y_conv = region_r[:, 3072:4096].rearrange("p (c t) -> p c t", c=4)
    y_conv_low = rounded("y_conv_low", [P, 4, S], "region_r", 3072)
    y_conv_high = rounded("y_conv_high", [P, 4, S], "ring", 12 * PIECE)
    z = region_r[:, 4096:4096 + 4 * (S + 2)].rearrange("p (c t) -> p c t", c=4)
    vx = ring[:, 12, 1024:2048].rearrange("p (t c) -> p t c", t=TT)
    flip = region_r[:, 3072:3072 + P]
    sig = [region_r[:, 5128 + 512 * n:5640 + 512 * n] for n in range(2)]
    rows = region_r[0:60, 5128:5256]
    table_hot = region_r[0:BUCKETS + 1, 5256:5264 + TOEP]
    table, hot = table_hot[:, 0:ATT_H], table_hot[:, ATT_H:]
    bias_of_dist = region_r[0:ATT_H, 5650:5650 + TOEP]
    squares2 = region_r[:, 2048:4096].rearrange("p (t d) -> p t d", t=TT)

    b_gu = region_r[:, 0:1024]
    b_down = region_r[0:E, 1024:2048]
    hidT = region_r[:, 1024:1536]
    xg = region_r[:, 2048:2560].rearrange("p (c s) -> p c s", c=KC)
    g_sb = region_r[:, 2560:3072]
    sg = region_r[:, 3072:3584]
    hid = region_r[:, 3584:4096]
    h2T = region_r[:, 2048:4096].rearrange("p (c t) -> p c t", c=KC)
    place = region_r[:, 4096:4096 + 2 * (STEPS + 1)].rearrange("p (t s) -> p t s", t=TT)
    wexp = region_r[:, 4354:4354 + 2 * (STEPS + 1)].rearrange("p (t s) -> p t s", t=TT)
    gat = region_r[:, 4612:4612 + TT * SLOTS].rearrange("p (t s) -> p t s", t=TT)
    sca = region_r[:, 4740:4740 + TT * P].rearrange("p (t s) -> p t s", t=TT)
    w_slot = region_r[:, 6132:6133]
    unused = region_r[:, 1536:1536 + TT * P]
    logit = region_r[:, 5316:5380].rearrange("p (t e) -> p t e", t=TT)
    mask = region_r[:, 5380:5444].rearrange("p (t e) -> p t e", t=TT)
    hit = region_r[:, 5444:5476]
    best = region_r[:, 5476:5492].rearrange("p (t k) -> p t k", t=TT)
    best_i = region_r[:, 5492:5508].rearrange("p (t k) -> p t k", t=TT)
    elog = region_r[:, 4612:4676].rearrange("p (t e) -> p t e", t=TT)
    gain_out = ring[:, 8, 0:D]
    rank = region_r[:, 5508:5572].rearrange("p (t e) -> p t e", t=TT)
    small = region_r[:, 5572:5588]
    w_rt = region_r[:, 5588:5844].rearrange("p (c e) -> p c e", c=KC)
    b_rt = region_r[:, 5844:5876]
    wexpT = region_r[0:E, 5876:6132]

    bank = [nc.alloc_psum_tensor(f"bank{n}", [P, 512], fp32) for n in range(8)]
    acc = [bank[0:2], bank[2:4]]
    gate_ps, lin_ps, tr_ps, y_ps = bank[4], bank[5], bank[6], bank[7]

    def sem(name):
        return ctx.enter_context(nc.semaphore(name))

    x_in = [sem(f"x_in{t}") for t in range(TT)]
    mem_in = [sem(f"mem_in{t}") for t in range(TT)]
    table_in, flip_in, rows_in, bias_in, scratch_out = sem("table_in"), sem("flip_in"), sem("rows_in"), sem("bias_in"), sem("scratch_out")
    x_again_in, expert_bias_in, router_in = sem("x_again_in"), sem("expert_bias_in"), sem("router_in")
    final_gain_in, out_done = sem("final_gain_in"), sem("out_done")
    piece_in = [sem(f"piece_in{n}") for n in range(RING)]
    down_in = [sem(f"down_in{n}") for n in range(DRING)]
    pieces_used, downs_used = sem("pieces_used"), sem("downs_used")
    cols_done, dist_done, bias_flipped = sem("cols_done"), sem("dist_done"), sem("bias_flipped")
    hT_done, scores_done = sem("hT_done"), sem("scores_done")
    probsT_done, pv_done, branch_done = sem("probsT_done"), sem("pv_done"), sem("branch_done")
    h2T_done, logits_done, rank_done = sem("h2T_done"), sem("logits_done"), sem("rank_done")
    wexpT_done, acc_open, acc_done = sem("wexpT_done"), sem("acc_open"), sem("acc_done")
    gathered, scaT_done, hidT_done, scattered = sem("gathered"), sem("scaT_done"), sem("hidT_done"), sem("scattered")
    w_high_ready, w_low_ready = sem("w_high_ready"), sem("w_low_ready")
    gained, act_high, hT_parts = sem("gained"), sem("act_high"), sem("hT_parts")
    conv_high, conv_parts, y_att_high_ready = sem("conv_high"), sem("conv_parts"), sem("y_att_high_ready")
    merged_high_ready, merged_parts = sem("merged_high_ready"), sem("merged_parts")
    cols_sb, dist_sb, mean_done, normed = sem("cols_sb"), sem("dist_sb"), sem("mean_done"), sem("normed")
    bias_sb = sem("bias_sb")
    proj_sb, att_scores_read, top_ready = sem("proj_sb"), sem("att_scores_read"), sem("top_ready")
    probs_ready, merged_sb, x2_sb, h2_sb, h2T_sb = sem("probs_ready"), sem("merged_sb"), sem("x2_sb"), sem("h2_sb"), sem("h2T_sb")
    best_ready, mask_sb, weights_sb, wexpT_sb = sem("best_ready"), sem("mask_sb"), sem("weights_sb"), sem("wexpT_sb")
    passes_ready = sem("passes_ready")
    gat_ready, sca_ready, sel_ready, xg_sb = sem("gat_ready"), sem("sca_ready"), sem("sel_ready"), sem("xg_sb")
    g_ready, up_read, hid_half, hid_ready = sem("g_ready"), sem("up_read"), sem("hid_half"), sem("hid_ready")
    b_parts_ready, scaT_sb, y_ready = sem("b_parts_ready"), sem("scaT_sb"), sem("y_ready")
    sum_ready, fin_sb, dve_step = sem("sum_ready"), sem("fin_sb"), sem("dve_step")
    sq_done, root_done, exp_done, probsT_sb = sem("sq_done"), sem("root_done"), sem("exp_done"), sem("probsT_sb")
    y_att_sb, gates_sb, router_exp = sem("y_att_sb"), sem("gates_sb"), sem("router_exp")
    sig_ready, hidT_sb, w_slot_ready, y_high = sem("sig_ready"), sem("hidT_sb"), sem("w_slot_ready"), sem("y_high")

    block = ctx.enter_context(nc.Block())

    @block.sync
    def _(sp):
        def mixer_piece(p, src, chunks):
            if p >= MIX_RING:
                sp.wait_ge(pieces_used, p - MIX_RING + 1)
            q = mixer_slot(p)
            sp.dma_start(ring[:, q, :].rearrange("p (c n) -> p c n", c=chunks), src).then_inc(piece_in[q], 16)

        sp.dma_start(table_hot, a["table_hot"]).then_inc(table_in, 16)
        for t in range(TT):
            sp.dma_start(mem_nat[:, t, :], a["mem"][0, t * P:(t + 1) * P, :]).then_inc(mem_in[t], 16)
        sp.dma_start(rows, a["rows"]).then_inc(rows_in, 16)
        sp.dma_start(consts[:, :], a["consts"][:, 0:C_KEPT]).then_inc(rows_in, 16)
        for t in range(TT):
            sp.dma_start(x_nat[:, t, :], a["x"][0, t * P:(t + 1) * P, :]).then_inc(x_in[t], 16)
        sp.dma_start(flip, a["consts"][:, C_KEPT:]).then_inc(flip_in, 16)
        p = 0
        for name, col in PROJ:
            if p == 3:
                sp.wait_ge(bias_in, 16)
            mixer_piece(p, a[name][0, :, col:col + 256].rearrange("(c p) n -> p c n", p=P), KC)
            p += 1
        for b, name, half in GROUPS:
            for j in range(2):
                col = GL + b * D + half * 512 + j * 256
                mixer_piece(p, a["w_in"][0, :, col:col + 256].rearrange("(c p) n -> p c n", p=P), KC)
                p += 1
            mixer_piece(p, a[name][0, :, half * 512:half * 512 + 512].rearrange("(c p) n -> p c n", p=P), 4)
            p += 1
        for j in range(4):
            mixer_piece(p, a["w_out"][0, j * 256:(j + 1) * 256, :].rearrange("(c p) n -> p c n", p=P), 2)
            p += 1
        sp.wait_ge(y_att_sb, ATT_H // 2 + X_H)
        sp.dma_start(x_again, a["x"][0].rearrange("(t p) d -> p t d", p=P)).then_inc(x_again_in, 16)

        def expert_up(expert, slot0, uses, chunks=range(KC)):
            for c in chunks:
                if uses is not None:
                    sp.wait_ge(pieces_used, uses + c)
                sp.dma_start(ring[:, slot0 + c, :],
                             a["w_gu"][0, bass.ds(expert, 1), c * P:(c + 1) * P, :].rearrange("e p n -> (e p) n"))\
                  .then_inc(piece_in[slot0 + c], 16)

        def expert_down(expert, uses):
            for j in range(DRING):
                if uses is not None:
                    sp.wait_ge(downs_used, uses + j)
                sp.dma_start(dring[:, j, :].rearrange("p (c n) -> p c n", c=2),
                             a["w_down"][0, bass.ds(expert, 1), j * 256:(j + 1) * 256, :]
                             .rearrange("e (c p) n -> p (e c) n", p=P)).then_inc(down_in[j], 16)

        expert_up(0, 8, N_MIX - MIX_RING + 1, range(MIX_RING - 8))
        expert_up(1, 0, N_MIX - 7)
        expert_up(0, 8, None, range(MIX_RING - 8, KC))
        expert_down(0, None)
        sp.wait_ge(passes_ready, 1)
        more = sp.value_load(more_i32[0:1, 0:1], min_val=0, max_val=PASSES - 1)
        with sp.Fori(0, more * (E // 2) + (E // 2 - 1 - IN_ORDER)) as i:
            expert_up((i * 2 + 2) % E, 8, i * 16 + (N_MIX - RING + 17))
            expert_down((i * 2 + 1) % E, i * 8 + 1)
            expert_up((i * 2 + 3) % E, 0, i * 16 + (N_MIX - RING + 25))
            expert_down((i * 2 + 2) % E, i * 8 + 5)
        ups, downs = more * (KC * E) + (N_MIX - RING + 1), more * (DRING * E) + (1 - DRING)
        e0 = E - 2 * IN_ORDER
        expert_down(e0 - 1, downs + DRING * (e0 - 1))
        with sp.Fori(0, IN_ORDER) as i:
            for u in range(2):
                e = i * 2 + (e0 + u)
                expert_up(e, 8 * (1 - u), ups + e * KC)
                expert_down(e, downs + e * DRING)
        sp.wait_ge(pieces_used, more * (KC * E) + (KC * (E - 1) + N_MIX))
        sp.dma_start(gain_out, a["norm_final_g"].unsqueeze(0).broadcast_to([P, D])).then_inc(final_gain_in, 16)
        for t in range(TT):
            sp.wait_ge(fin_sb, t + 1)
            sp.dma_start(out[0, t * P:(t + 1) * P, :], x2[:, t, :]).then_inc(out_done, 16)
        sp.wait_ge(out_done, 16 * TT)

    @block.gpsimd
    def _(pool):
        pool.wait_ge(dist_sb, 1)
        pool.dma_start(scratch[:, 0:TOEP], bias_of_dist).then_inc(scratch_out, 16)
        pool.wait_ge(scratch_out, 16)
        pool.dma_start(bias, bass.AP(scratch.tensor, 0, [[1, P], [384, ATT_H], [1, 2 * P]])).then_inc(bias_in, 16)
        pool.wait_ge(merged_sb, 2 * len(GROUPS))
        pool.dma_start(w_rt, a["w_router"][0].rearrange("(c p) e -> p c e", p=P)).then_inc(router_in, 16)
        pool.dma_start(b_rt, a["b_router"].broadcast_to([P, E])).then_inc(router_in, 16)
        pool.wait_ge(pieces_used, N_MIX)
        for q in range(4):
            half = q % 2
            pool.dma_start(b_gu[q * E:(q + 1) * E, :].rearrange("e (k n) -> e k n", k=2),
                           a["b_gu"][0].rearrange("e (k h n) -> e k h n", k=2, h=2)[:, :, half, :])\
                .then_inc(expert_bias_in, 16)
        pool.dma_start(b_down, a["b_down"][0]).then_inc(expert_bias_in, 16)

    @block.scalar
    def _(act):
        act.wait_ge(mean_done, 1)
        act.activation(norm[:, 0, 4:6], norm[:, 0, 2:4], ACT.Sqrt)

        def square_sums(src, into, n, t):
            act.activation(into[:, t, :], src[:, t, :], ACT.Square, accum_out=norm[:, n, t:t + 1]).then_inc(sq_done, 1)

        def root(n):
            act.wait_ge(mean_done, n + 2)
            act.activation(norm[:, n, 4:6], norm[:, n, 2:4], ACT.Sqrt).then_inc(root_done, 1)

        def w_high_part(p):
            if p >= N_MIX:
                return
            q = mixer_slot(p)
            act.wait_ge(piece_in[q], 16 * mixer_loads(p))
            if p >= 3:
                act.wait_ge(pieces_used, p - 2)
            act.activation(w_high[p % 3][:, :], ring[:, q, :], ACT.Copy).then_inc(w_high_ready, 1)

        def act_high_part(u, src, dst):
            act.wait_ge(gained, u + 1)
            t, half = u % 4 // 2, u % 2
            cut = (slice(None), slice(4 * half, 4 * half + 4), slice(t * P, (t + 1) * P))
            act.activation(dst[cut], src[cut], ACT.Copy).then_inc(act_high, 1)

        for t in range(TT):
            act.wait_ge(mem_in[t], 16)
            square_sums(mem_nat, squares, 0, t)
        root(0)
        act.wait_ge(sq_done, TT)
        for t in range(TT):
            act.wait_ge(x_in[t], 16)
            square_sums(x_nat, squares, 1, t)
        for u in range(4):
            act_high_part(u, memT, memT_high)
        act.wait_ge(sq_done, 2 * TT)
        w_high_part(0)
        root(1)
        w_high_part(1)
        w_high_part(2)

        def exp(hh):
            act.wait_ge(top_ready, hh + 1)
            pr = probs[hh % 2]
            if hh < ATT_H:
                for n, cut in enumerate((slice(0, 256), slice(256, 384))):
                    last = act.activation(pr[:, cut], pr[:, cut], ACT.Exp, bias=negtop[:, hh, n:n + 1],
                                          accum_out=sums[:, hh, n:n + 1])
            else:
                act.wait_ge(probsT_done, hh - 1)
                for n in range(TT):
                    cut = slice(n * 256, n * 256 + 256)
                    last = act.activation(pr[:, cut], bank[2 + hh % 2][:, cut], ACT.Exp,
                                          bias=negtop[:, hh, n:n + 1], scale=X_D ** -0.5,
                                          accum_out=sums[:, hh, n:n + 1])
            last.then_inc(exp_done, 1)

        def probsT_copy(hh):
            act.wait_ge(probsT_done, hh + 1)
            n = 384 if hh < ATT_H else 512
            act.activation(probsT[hh % 2][:, 0:n], bank[4][:, 0:n], ACT.Copy).then_inc(probsT_sb, 1)

        def pv_high(hh):
            if hh < ATT_H and hh % 2 == 0:
                return
            u, dst = ((hh // 2, y_att_high[:, hh // 2, :]) if hh < ATT_H else
                      (hh - ATT_H // 2, y_x_high[:, hh - ATT_H, :]))
            act.wait_ge(pv_done, u + 1)
            act.activation(dst, bank[5][:, 0:256], ACT.Copy).then_inc(y_att_high_ready, 1)

        def heads(j):
            if 0 <= j - 2 < HEADS:
                probsT_copy(j - 2)
            if 0 <= j - 3 < HEADS:
                pv_high(j - 3)
            if 0 <= j < HEADS:
                exp(j)

        for p in range(N_PROJ):
            w_high_part(p + 3)
            if p == 0:
                for u in range(4):
                    act_high_part(4 + u, hT, hT_high)
            if PROJ[p][0] == "w_in" and CB <= PROJ[p][1] < CC:
                k = (PROJ[p][1] - CB) // P
                act.wait_ge(proj_sb, p + 1)
                act.activation(y_conv_high[:, k:k + 2, :], y_conv[:, k:k + 2, :], ACT.Copy).then_inc(conv_high, 1)
            heads(p - FIRST_HEAD)

        def sigmoid(n):
            b, _, half = GROUPS[n // 2]
            act.wait_ge(pieces_used, N_PROJ + 3 * (n // 2) + n % 2 + 1)
            if n >= 2:
                act.wait_ge(merged_sb, n - 1)
            for k in range(2):
                tile = b * 8 + half * 4 + (n % 2) * 2 + k
                last = act.activation(sig[n % 2][:, k * 256:k * 256 + 256], bank[n % 2][:, k * 256:k * 256 + 256],
                                      ACT.Sigmoid, bias=b_gate[:, tile:tile + 1])
            last.then_inc(gates_sb, 1)

        def merged_high_part(n):
            if n < 8:
                return
            tile = merged_tile(n)
            act.wait_ge(merged_sb, n + 1)
            act.activation(merged_high[:, tile:tile + 2, :], merged[:, tile:tile + 2, :], ACT.Copy)\
                .then_inc(merged_high_ready, 1)

        for g in range(len(GROUPS)):
            p = N_PROJ + 3 * g
            sigmoid(2 * g)
            w_high_part(p + 3)
            heads(ATT_H + 2 * g)
            sigmoid(2 * g + 1)
            w_high_part(p + 4)
            heads(ATT_H + 2 * g + 1)
            merged_high_part(2 * g)
            w_high_part(p + 5)
            merged_high_part(2 * g + 1)
        w_high_part(N_MIX - 1)

        for t in range(TT):
            act.wait_ge(x2_sb, t + 1)
            square_sums(x2, squares2, 2, t)
        root(2)
        act.wait_ge(best_ready, 1)
        for t in range(TT):
            last = act.activation(elog[:, t, :], logit[:, t, :], ACT.Exp, bias=small[:, t:t + 1])
        last.then_inc(router_exp, 1)

        act.wait_ge(passes_ready, 1)
        more = act.value_load(more_i32[0:1, 0:1], min_val=0, max_val=PASSES - 1)
        with act.Fori(0, more * (E // 2) + E // 2) as i:
            for u in range(2):
                s = i * 2 + u
                act.wait_ge(g_ready, s + 1)
                act.activation(sg, g_sb, ACT.Sigmoid, scale=ALPHA).then_inc(sig_ready, 1)
                act.wait_ge(scaT_done, s + 1)
                act.wait_ge(y_ready, s + 1)
                act.activation(unused, y_ps[:, 0:TT * P], ACT.Copy, accum_out=w_slot).then_inc(w_slot_ready, 1)
                act.wait_ge(hidT_done, s + 1)
                act.activation(hidT, tr_ps[:, :], ACT.Copy).then_inc(hidT_sb, 1)
                act.wait_ge(downs_used, (s + 1) * DRING)
                act.wait_ge(w_slot_ready, s + 1)
                act.activation(y_parts[0:64, 0:512], y_ps[0:64, :], ACT.Copy, scale=w_slot[0:64, :])
                act.activation(y_parts[64:128, 512:1024], y_ps[64:128, :], ACT.Copy, scale=w_slot[64:128, :])\
                    .then_inc(y_high, 1)

        for t in range(TT):
            act.wait_ge(sum_ready, t + 1)
            square_sums(x2, h2, 3, t)
            act.wait_ge(mean_done, 5 + t)
            act.activation(norm[:, 3, 4 + t:5 + t], norm[:, 3, 2 + t:3 + t], ACT.Sqrt).then_inc(root_done, 1)

    @block.vector
    def _(dve):
        steps = [0]

        def link(ins):
            steps[0] += 1
            ins.then_inc(dve_step, 1)
            dve.wait_ge(dve_step, steps[0])

        dve.memset(norm[:, 0, 2:4], 1.0).then_inc(mean_done, 1)
        dve.memset(ones[:, :], 1.0)
        dve.memset(z[:, :, 0:2], 0.0)

        def rstd(n):
            dve.wait_ge(sq_done, TT * (n + 1))
            dve.tensor_scalar(norm[:, n, 2:4], norm[:, n, 0:2], 1.0 / D, EPS, ALU.mult, ALU.add).then_inc(mean_done, 1)
            dve.wait_ge(root_done, n + 1)
            link(dve.reciprocal(norm[:, n, 6:8], norm[:, n, 4:6]))

        def normalise(n, src, dst, done):
            for t in range(TT):
                dve.tensor_scalar(dst[:, t, :], src[:, t, :], norm[:, n, 6 + t:7 + t], None, ALU.mult).then_inc(done, 1)

        def with_gain(ps, gain, dst, half, t, done):
            g4 = gain[:, 4 * half:4 * half + 4].unsqueeze(2).broadcast_to([P, 4, P])
            dve.tensor_tensor(dst[:, 4 * half:4 * half + 4, t * P:(t + 1) * P],
                              ps[:, :].rearrange("p (c t) -> p c t", c=4), g4, ALU.mult).then_inc(done, 1)

        dve.wait_ge(dist_done, 1)
        dve.tensor_copy(bias_of_dist, bank[3][0:ATT_H, 0:TOEP]).then_inc(dist_sb, 1)
        dve.wait_ge(cols_done, 1)
        dve.tensor_copy(cols[:, :], bank[2][:, 0:60]).then_inc(cols_sb, 1)
        def act_low_parts(u0, src, high, low):
            for u in range(u0, u0 + 4):
                dve.wait_ge(act_high, u + 1)
                t, half = u % 4 // 2, u % 2
                cut = (slice(None), slice(4 * half, 4 * half + 4), slice(t * P, (t + 1) * P))
                dve.tensor_tensor(low[cut], src[cut], high[cut].bitcast(fp32), ALU.subtract).then_inc(hT_parts, 1)

        def w_low_part(p):
            if p >= N_MIX:
                return
            q = mixer_slot(p)
            dve.wait_ge(w_high_ready, p + 1)
            dve.tensor_tensor(w_low[q][:, :], ring[:, q, :], w_high[p % 3][:, :].bitcast(fp32), ALU.subtract)\
                .then_inc(w_low_ready, 1)

        rstd(0)
        normalise(0, mem_nat, mem_nat, normed)
        dve.wait_ge(cols_sb, 1)
        for u in range(4):
            dve.wait_ge(hT_done, u + 1)
            with_gain(bank[4 + u], g_mem, memT, u % 2, u // 2, gained)
        act_low_parts(0, memT, memT_high, memT_low)
        w_low_part(0)
        rstd(1)
        normalise(1, x_nat, x_nat, normed)
        w_low_part(1)
        w_low_part(2)

        def projection(u):
            dve.wait_ge(pieces_used, u + 1)
            ps = bank[u % 2][:, :].rearrange("p (k t) -> p k t", k=2)
            name, col = PROJ[u]
            if name == "w_mem_kv":
                j = col // 256
                ins = (dve.tensor_copy(kx[:, 2 * j:2 * j + 2, :], ps) if j < 2 else
                       dve.tensor_copy(vx[:, :, (j - 2) * 256:(j - 1) * 256], ps))
            elif col < VA:
                ins = dve.tensor_copy(qk[:, col // P:col // P + 2, :], ps)
            elif col < CB:
                ins = dve.tensor_copy(v_att[:, :, col - VA:col - VA + 256], ps)
            elif col >= QX:
                ins = dve.tensor_copy(qx[:, (col - QX) // P:(col - QX) // P + 2, :], ps)
            elif col >= CU:
                k = (col - CU) // P
                dve.wait_ge(proj_sb, u - 1)
                ins = dve.tensor_tensor(z[:, k:k + 2, 2:], ps, z[:, k:k + 2, 2:], ALU.mult)
            elif col >= CC:
                k = (col - CC) // P
                ins = dve.tensor_copy(z[:, k:k + 2, 2:], ps)
            else:
                k = (col - CB) // P
                ins = dve.tensor_tensor(y_conv[:, k:k + 2, :], ps, y_conv[:, k:k + 2, :], ALU.mult)
            ins.then_inc(proj_sb, 1)
            if name == "w_in" and CU <= col < QX:
                dve.wait_ge(proj_sb, u + 1)
                for c in range(k, k + 2):
                    link(dve.tensor_scalar(y_conv[:, c, :], z[:, c, 0:S], conv_w[:, c:c + 1], None, ALU.mult))
                    for tap in (1, 2):
                        w = conv_w[:, 4 * tap + c:4 * tap + c + 1]
                        link(dve.scalar_tensor_tensor(y_conv[:, c, :], z[:, c, tap:tap + S], w, y_conv[:, c, :],
                                                      ALU.mult, ALU.add))

        def head_top(hh):
            dve.wait_ge(scores_done, hh + 1)
            ps, pr = bank[2 + hh % 2], probs[hh % 2]
            if hh < ATT_H:
                if hh == 0:
                    dve.wait_ge(bias_sb, 4)
                if hh >= 2:
                    dve.wait_ge(probsT_done, hh - 1)
                dve.scalar_tensor_tensor(pr[:, 0:256], ps[:, 0:256], ATT_D ** -0.5, bias[:, hh, :], ALU.mult, ALU.add)
                dve.scalar_tensor_tensor(pr[:, 256:384], ps[:, 256:384], ATT_D ** -0.5, bias[:, hh, 128:256],
                                         ALU.mult, ALU.add).then_inc(att_scores_read, 1)
                dve.wait_ge(att_scores_read, hh + 1)
                dve.tensor_reduce(top[:, hh, 0:1], pr[:, 0:256], AX.X, ALU.max)
                link(dve.tensor_reduce(top[:, hh, 1:2], pr[:, 256:384], AX.X, ALU.max))
                scale = 1.0
            else:
                link(dve.tensor_reduce(top[:, hh, :], ps[:, :].rearrange("p (t k) -> p t k", t=TT), AX.X, ALU.max))
                scale = X_D ** -0.5
            dve.tensor_scalar(negtop[:, hh, :], top[:, hh, :], -scale, None, ALU.mult).then_inc(top_ready, 1)

        def head_norm(hh):
            dve.wait_ge(exp_done, hh + 1)
            link(dve.reciprocal(top[:, hh, :], sums[:, hh, :]))
            pr = probs[hh % 2]
            cuts = (slice(0, 256), slice(256, 384 if hh < ATT_H else 512))
            for n, cut in enumerate(cuts):
                last = dve.tensor_scalar(pr[:, cut], pr[:, cut], top[:, hh, n:n + 1], None, ALU.mult)
            last.then_inc(probs_ready, 1)

        def pv_low(hh):
            if hh < ATT_H and hh % 2 == 0:
                return
            u = hh // 2 if hh < ATT_H else hh - ATT_H // 2
            high, low, k = (y_att_high, y_att_low, hh // 2) if hh < ATT_H else (y_x_high, y_x_low, hh - ATT_H)
            dve.wait_ge(y_att_high_ready, u + 1)
            dve.tensor_tensor(low[:, k, :], bank[5][:, 0:256], high[:, k, :].bitcast(fp32), ALU.subtract)\
                .then_inc(y_att_sb, 1)

        def heads_before(j):
            if 0 <= j - 4 < HEADS:
                pv_low(j - 4)
            if 0 <= j - 1 < HEADS:
                head_norm(j - 1)

        for p in range(N_PROJ):
            heads_before(p - FIRST_HEAD)
            projection(p)
            w_low_part(p + 3)
            if p == 0:
                for u in range(4):
                    dve.wait_ge(hT_done, 4 + u + 1)
                    with_gain(bank[4 + u], g_mix, hT, u % 2, u // 2, gained)
                act_low_parts(4, hT, hT_high, hT_low)
            if p == 3:
                for j in range(4):
                    dve.wait_ge(bias_flipped, j + 1)
                    dve.tensor_copy(bias[:, 2 * j:2 * j + 2, :], bank[2 + j % 2][:, :].rearrange("p (h k) -> p h k", h=2))\
                        .then_inc(bias_sb, 1)
            if PROJ[p - 1][0] == "w_in" and CB <= PROJ[p - 1][1] < CC:
                k = (PROJ[p - 1][1] - CB) // P
                dve.wait_ge(conv_high, k // 2 + 1)
                dve.tensor_tensor(y_conv_low[:, k:k + 2, :], y_conv[:, k:k + 2, :],
                                  y_conv_high[:, k:k + 2, :].bitcast(fp32), ALU.subtract).then_inc(conv_parts, 1)
            if p >= FIRST_HEAD:
                head_top(p - FIRST_HEAD)

        def combine(n):
            g = n // 2
            tile = merged_tile(n)
            dst = merged[:, tile:tile + 2, :].rearrange("p c t -> p (c t)")
            dve.wait_ge(gates_sb, n + 1)
            if n % 2:
                dve.wait_ge(pieces_used, N_PROJ + 3 * g + 3)
            else:
                dve.wait_ge(branch_done, g + 1)
            if g < 2:
                dve.tensor_tensor(dst, bank[6 + n % 2][:, :], sig[n % 2], ALU.mult).then_inc(merged_sb, 1)
            else:
                link(dve.tensor_tensor(sig[n % 2], bank[6 + n % 2][:, :], sig[n % 2], ALU.mult))
                dve.wait_ge(merged_sb, n)
                dve.tensor_tensor(dst, dst, sig[n % 2], ALU.add).then_inc(merged_sb, 1)

        def merged_low_part(n):
            if n < 8:
                return
            tile = merged_tile(n)
            dve.wait_ge(merged_high_ready, n - 7)
            dve.tensor_tensor(merged_low[:, tile:tile + 2, :], merged[:, tile:tile + 2, :],
                              merged_high[:, tile:tile + 2, :].bitcast(fp32), ALU.subtract).then_inc(merged_parts, 1)

        for g in range(len(GROUPS)):
            p = N_PROJ + 3 * g
            for u in range(2):
                j = ATT_H + 2 * g + u
                heads_before(j)
                if u == 0:
                    w_low_part(p + 3)
                if j < HEADS:
                    head_top(j)
                if u == 0:
                    w_low_part(p + 4)
                    combine(2 * g)
            merged_low_part(2 * g)
            combine(2 * g + 1)
            w_low_part(p + 5)
            merged_low_part(2 * g + 1)
        w_low_part(N_MIX - 1)

        dve.wait_ge(x_again_in, 16)
        dve.wait_ge(pieces_used, N_MIX)
        for t in range(TT):
            for half in range(2):
                cut = slice(half * 512, half * 512 + 512)
                last = dve.tensor_tensor(x2[:, t, cut], bank[2 + 2 * t + half][:, :], x_again[:, t, cut], ALU.add)
            last.then_inc(x2_sb, 1)
        rstd(2)
        dve.wait_ge(x2_sb, TT)
        normalise(2, x2, h2, h2_sb)
        for u in range(4):
            dve.wait_ge(h2T_done, u + 1)
            with_gain(bank[(6, 7, 0, 1)[u]], g_ffn, h2T, u % 2, u // 2, h2T_sb)

        dve.wait_ge(router_in, 32)
        dve.wait_ge(logits_done, 1)
        link(dve.tensor_tensor(logit, bank[4][:, 0:TT * E].rearrange("p (t e) -> p t e", t=TT),
                               b_rt.unsqueeze(1).broadcast_to([P, TT, E]), ALU.add))
        dve.max(best[:, 0, :], logit[:, 0, :])
        link(dve.max(best[:, 1, :], logit[:, 1, :]))
        dve.tensor_scalar(small[:, 0:2], best[:, :, 0], -1.0, None, ALU.mult).then_inc(best_ready, 1)
        dve.max_index(best_u[:, 0, :], best[:, 0, :], logit[:, 0, :])
        link(dve.max_index(best_u[:, 1, :], best[:, 1, :], logit[:, 1, :]))
        link(dve.tensor_copy(best_i, best_u[:, :, :]))
        for k in range(TOPK):
            for t in range(TT):
                if k == 0:
                    last = dve.tensor_scalar(mask[:, t, :], slot_no[:, 0:E], best_i[:, t, 0:1], None, ALU.is_equal)
                else:
                    last = dve.scalar_tensor_tensor(mask[:, t, :], slot_no[:, 0:E], best_i[:, t, k:k + 1],
                                                    mask[:, t, :], ALU.is_equal, ALU.add)
            if k < TOPK - 1:
                link(last)
        last.then_inc(mask_sb, 1)

        dve.wait_ge(router_exp, 1)
        dve.wait_ge(mask_sb, 1)
        link(dve.tensor_tensor(elog, elog, mask, ALU.mult))
        link(dve.tensor_reduce(small[:, 2:4], elog, AX.X, ALU.add))
        link(dve.reciprocal(small[:, 4:6], small[:, 2:4]))
        for t in range(TT):
            for b in range(PASSES):
                last = dve.tensor_scalar(wexp[:, t, b * E:(b + 1) * E], elog[:, t, :], small[:, 4 + t:5 + t], None, ALU.mult)
        dve.memset(wexp[:, :, STEPS:], 0.0)
        last = dve.memset(place[:, :, STEPS:], -1.0)
        last.then_inc(weights_sb, 1)

        dve.wait_ge(rank_done, 1)
        link(dve.scalar_tensor_tensor(rank, bank[5][:, 0:TT * E].rearrange("p (t e) -> p t e", t=TT), 1.0, mask,
                                      ALU.add, ALU.mult))
        for b in range(PASSES):
            dve.tensor_scalar(place[:, :, b * E:(b + 1) * E], rank, -1.0 - SLOTS * b, None, ALU.add)
        link(dve.tensor_reduce(small[:, 6:7], bank[5][:, TT * E:(TT + 1) * E], AX.X, ALU.max))
        link(dve.tensor_scalar(small[:, 7:8], small[:, 6:7], float(SLOTS), None, ALU.is_gt))
        for b in range(2, PASSES):
            link(dve.scalar_tensor_tensor(small[:, 6 + b:7 + b], small[:, 6:7], float(SLOTS * b),
                                          small[:, 5 + b:6 + b], ALU.is_gt, ALU.add))
        dve.tensor_copy(more_i32[0:1, 0:1], small[0:1, 5 + PASSES:6 + PASSES]).then_inc(passes_ready, 1)
        dve.wait_ge(wexpT_done, 1)
        dve.tensor_copy(wexpT, bank[6][0:E, 0:TT * P]).then_inc(wexpT_sb, 1)

        def gather_matrix(s):
            for t in range(TT):
                last = dve.tensor_scalar(gat[:, t, :], slot_no[:, 0:SLOTS], place[:, t, bass.ds(s, 1)], None, ALU.is_equal)
            last.then_inc(gat_ready, 1)

        def scatter_matrix(s):
            for t in range(TT):
                last = dve.tensor_scalar(sca[:, t, :], slot_no, place[:, t, bass.ds(s, 1)], wexp[:, t, bass.ds(s, 1)],
                                         ALU.is_equal, ALU.mult)
            last.then_inc(sca_ready, 1)

        def bias_selector(s):
            dve.tensor_scalar(sel[:, :], half_of, pick[:, bass.ds(s, 1)], None, ALU.mult).then_inc(sel_ready, 1)

        gather_matrix(0)
        scatter_matrix(0)
        bias_selector(0)
        dve.wait_ge(acc_open, 1)
        dve.wait_ge(expert_bias_in, 16 * 5)
        dve.tensor_copy(b_parts[0:64, :], b_gu[0:64, :])
        link(dve.tensor_copy(y_parts[64:128, :], b_gu[64:128, :]))
        dve.tensor_tensor(b_parts[64:128, :], b_gu[64:128, :], y_parts[64:128, :].bitcast(fp32), ALU.subtract)\
            .then_inc(b_parts_ready, 1)
        dve.wait_ge(b_parts_ready, 1)
        link(dve.memset(zero[:, :], 0.0))
        dve.tensor_copy(scaT[:, :, :].rearrange("p t s -> p (t s)"), zero[:, 0:1].broadcast_to([P, TT * P])).then_inc(scaT_sb, 1)
        dve.tensor_copy(y_parts[:, :], zero[:, 0:1].broadcast_to([P, 1024])).then_inc(y_ready, 1)
        dve.memset(hidT[:, 0:2], 0.0).then_inc(hidT_sb, 1)
        dve.memset(g_sb[:, 0:2], 0.0).then_inc(up_read, 1)
        dve.wait_ge(gathered, 1)
        dve.tensor_tensor(xg, tr_ps[:, :].rearrange("p (c s) -> p c s", c=KC),
                          g_ffn.unsqueeze(2).broadcast_to([P, KC, SLOTS]), ALU.mult).then_inc(xg_sb, 1)

        more = dve.value_load(more_i32[0:1, 0:1], min_val=0, max_val=PASSES - 1)
        with dve.Fori(0, more * (E // 2) + E // 2) as i:
            for u in range(2):
                s = i * 2 + u
                dve.wait_ge(gathered, s + 1)
                gather_matrix(s + 1)
                dve.wait_ge(pieces_used, (s + 1) * KC + N_MIX)
                dve.tensor_scalar(g_sb, gate_ps[:, :], LIMIT, None, ALU.min).then_inc(g_ready, 1)
                dve.tensor_scalar(hid, lin_ps[:, :], LIMIT, -LIMIT, ALU.min, ALU.max).then_inc(up_read, 1)
                dve.wait_ge(g_ready, s + 1)
                dve.wait_ge(up_read, s + 2)
                dve.scalar_tensor_tensor(hid, hid, 1.0, g_sb, ALU.add, ALU.mult).then_inc(hid_half, 1)
                dve.wait_ge(hid_half, s + 1)
                dve.wait_ge(sig_ready, s + 1)
                dve.tensor_tensor(hid, hid, sg, ALU.mult).then_inc(hid_ready, 1)
                dve.wait_ge(w_slot_ready, s + 1)
                dve.wait_ge(scattered, s + 1)
                dve.tensor_scalar(scaT[:, :, :].rearrange("p t s -> p (t s)"), y_ps[:, 0:TT * P], 0.0, None, ALU.not_equal)\
                    .then_inc(scaT_sb, 1)
                bias_selector(s + 1)
                dve.wait_ge(gathered, s + 2)
                dve.tensor_tensor(xg, tr_ps[:, :].rearrange("p (c s) -> p c s", c=KC),
                                  g_ffn.unsqueeze(2).broadcast_to([P, KC, SLOTS]), ALU.mult).then_inc(xg_sb, 1)
                scatter_matrix(s + 1)
                dve.wait_ge(downs_used, (s + 1) * DRING)
                dve.wait_ge(y_high, s + 1)
                dve.scalar_tensor_tensor(y_parts[64:128, 0:512], y_ps[0:64, :], w_slot[0:64, :],
                                         y_parts[0:64, 0:512].bitcast(fp32), ALU.mult, ALU.subtract)
                dve.scalar_tensor_tensor(y_parts[0:64, 512:1024], y_ps[64:128, :], w_slot[64:128, :],
                                         y_parts[64:128, 512:1024].bitcast(fp32), ALU.mult, ALU.subtract)\
                    .then_inc(y_ready, 1)

        dve.wait_ge(acc_done, 1)
        dve.wait_ge(final_gain_in, 16)
        for t in range(TT):
            for half in range(2):
                cut = slice(half * 512, half * 512 + 512)
                last = dve.tensor_tensor(x2[:, t, cut], acc[t][half][:, :], x2[:, t, cut], ALU.add)
            last.then_inc(sum_ready, 1)
        for t in range(TT):
            dve.wait_ge(sq_done, 3 * TT + t + 1)
            dve.tensor_scalar(norm[:, 3, 2 + t:3 + t], norm[:, 3, t:t + 1], 1.0 / D, EPS, ALU.mult, ALU.add)\
                .then_inc(mean_done, 1)
            dve.wait_ge(root_done, 4 + t)
            link(dve.reciprocal(norm[:, 3, 6 + t:7 + t], norm[:, 3, 4 + t:5 + t]))
            dve.scalar_tensor_tensor(x2[:, t, :], x2[:, t, :], norm[:, 3, 6 + t:7 + t], gain_out, ALU.mult, ALU.mult)\
                .then_inc(fin_sb, 1)

    @block.tensor
    def _(pe):
        mm, transpose = pe.matmul, pe.transpose

        def parts(p, chunks):
            pe.wait_ge(w_low_ready, p + 1)
            return [w.rearrange("p (c n) -> p c n", c=chunks) for w in (w_high[p % 3][:, :], w_low[mixer_slot(p)][:, :])]

        def product(dst, lhsT, rhs, at_l, at_r, first, last):
            for n, (l, r) in enumerate(((0, 0), (0, 1), (1, 0))):
                ins = mm(dst, lhsT[l][at_l], rhs[r][at_r], start=first and n == 0, stop=last and n == 2)
            return ins

        def transposed(src, u, out_bank, done):
            t, half = u // 2, u % 2
            for c in range(4):
                last = transpose(out_bank[:, c * P:(c + 1) * P], src[:, t, (4 * half + c) * P:(4 * half + c + 1) * P], ident)
            last.then_inc(done, 1)

        pe.wait_ge(table_in, 16)
        mm(bank[3][0:ATT_H, 0:TOEP], table, hot, start=True, stop=True).then_inc(dist_done, 1)
        pe.wait_ge(rows_in, 16 * 2)
        transpose(bank[2][:, 0:60], rows, ident[0:60, 0:60]).then_inc(cols_done, 1)
        for u in range(4):
            pe.wait_ge(normed, u // 2 + 1)
            transposed(mem_nat, u, bank[4 + u], hT_done)

        def projection(u):
            if u >= 2:
                pe.wait_ge(proj_sb, u - 1)
            w = parts(u, KC)
            name, col = PROJ[u]
            src = (hT_high, hT_low) if name == "w_in" else (memT_high, memT_low)
            values = VA <= col < CB if name == "w_in" else col >= 512
            for k in range(2):
                dst, cut = bank[u % 2][:, k * 256:k * 256 + 256], slice(k * P, k * P + P)
                for c in range(KC):
                    narrow, wide = (slice(None), c, cut), (slice(None), c, slice(0, 256))
                    lhsT, rhs = (src, w) if values else (w, src)
                    last = product(dst, lhsT, rhs, narrow, wide, c == 0, c == KC - 1)
            last.then_inc(pieces_used, 1)

        def scores(hh):
            dst = bank[2 + hh % 2]
            if hh < ATT_H:
                if hh >= 2:
                    pe.wait_ge(att_scores_read, hh - 1)
                else:
                    pe.wait_ge(bias_sb, 3 + hh)
                q = qk[64 * (hh % 2):64 * (hh % 2) + 64, hh // 2, :]
                k = qk[64 * (hh % 2):64 * (hh % 2) + 64, 4 + hh // 2, :]
                mm(dst[:, 0:256], q[:, P:2 * P], k, start=True, stop=True)
                mm(dst[:, 256:384], q[:, 0:P], k[:, 0:P], start=True, stop=True).then_inc(scores_done, 1)
            else:
                if hh < ATT_H + 2:
                    pe.wait_ge(att_scores_read, hh - 1)
                else:
                    pe.wait_ge(exp_done, hh - 1)
                for t in range(TT):
                    last = mm(dst[:, t * 256:t * 256 + 256], qx[:, hh - ATT_H, t * P:(t + 1) * P], kx[:, hh - ATT_H, :],
                              start=True, stop=True)
                last.then_inc(scores_done, 1)

        def probs_transposed(hh):
            pe.wait_ge(probs_ready, hh + 1)
            if hh:
                pe.wait_ge(probsT_sb, hh)
            pr, dst = probs[hh % 2], bank[4]
            moves = ([(0, 256), (128, 0), (256, 128)] if hh < ATT_H else
                     [(k * 256 + t * P, t * 256 + k * P) for k in range(2) for t in range(TT)])
            for to, at in moves:
                last = transpose(dst[:, to:to + P], pr[:, at:at + P], ident)
            last.then_inc(probsT_done, 1)

        def values(hh):
            pe.wait_ge(probsT_sb, hh + 1)
            pT = probsT[hh % 2]
            u = hh // 2 if hh < ATT_H else hh - ATT_H // 2
            if u:
                pe.wait_ge(y_att_sb, u)
            if hh < ATT_H:
                dst = bank[5][64 * (hh % 2):64 * (hh % 2) + 64, 0:256]
                mm(dst, v_att[:, 0, 64 * hh:64 * hh + 64], pT[:, 0:256], start=True, stop=False)
                last = mm(dst[:, P:2 * P], v_att[:, 1, 64 * hh:64 * hh + 64], pT[:, 256:384], start=False, stop=True)
                if hh % 2:
                    last.then_inc(pv_done, 1)
            else:
                x = hh - ATT_H
                dst = bank[5][:, 0:256]
                for k in range(2):
                    last = mm(dst, vx[:, k, x * P:(x + 1) * P], pT[:, k * 256:k * 256 + 256], start=(k == 0), stop=(k == 1))
                last.then_inc(pv_done, 1)

        def heads(j):
            if 0 <= j < HEADS:
                scores(j)
            if 0 <= j - 2 < HEADS:
                probs_transposed(j - 2)
            if 0 <= j - 3 < HEADS:
                values(j - 3)

        pe.wait_ge(hT_parts, 4)
        for p in range(N_PROJ):
            if p == 4:
                pe.wait_ge(hT_parts, 8)
            projection(p)
            if p == 0:
                for u in range(4):
                    pe.wait_ge(normed, TT + u // 2 + 1)
                    transposed(x_nat, u, bank[4 + u], hT_done)
            if p == 3:
                pe.wait_ge(bias_in, 16)
                pe.wait_ge(flip_in, 16)
                pe.wait_ge(cols_sb, 1)
                pe.wait_ge(dist_sb, 1)
                for j in range(4):
                    if j >= 2:
                        pe.wait_ge(bias_sb, j - 1)
                    mm(bank[2 + j % 2][:, :], flip, bias[:, 2 * j:2 * j + 2, :].rearrange("p h k -> p (h k)"),
                       start=True, stop=True).then_inc(bias_flipped, 1)
            heads(p - FIRST_HEAD)

        def gate_logits(n):
            w = parts(N_PROJ + 3 * (n // 2) + n % 2, KC)
            if n < 2:
                pe.wait_ge(proj_sb, N_PROJ - 1 + n)
            else:
                pe.wait_ge(gates_sb, n - 1)
            for k in range(2):
                for c in range(KC):
                    last = product(bank[n % 2][:, k * 256:k * 256 + 256], w, (hT_high, hT_low),
                                   (slice(None), c, slice(k * P, (k + 1) * P)), (slice(None), c, slice(0, S)),
                                   c == 0, c == KC - 1)
            last.then_inc(pieces_used, 1)

        def branch(g, second):
            b = GROUPS[g][0]
            w = parts(N_PROJ + 3 * g + 2, 4)
            y = {1: (y_conv_high, y_conv_low), 0: (y_att_high, y_att_low), 2: (y_x_high, y_x_low)}[b]
            if b == 1:
                pe.wait_ge(conv_parts, 2)
            else:
                pe.wait_ge(y_att_sb, ATT_H // 2 + (X_H if b == 2 else 0))
            if g:
                pe.wait_ge(merged_sb, 2 * g - 1 + second)
            for k in range(2):
                at = (2 * second + k) * P
                for c in range(4):
                    last = product(bank[6 + second][:, k * 256:k * 256 + 256], w, y,
                                   (slice(None), c, slice(at, at + P)), (slice(None), c, slice(0, S)), c == 0, c == 3)
            last.then_inc(pieces_used if second else branch_done, 1)

        for g in range(len(GROUPS)):
            gate_logits(2 * g)
            heads(ATT_H + 2 * g)
            gate_logits(2 * g + 1)
            branch(g, 0)
            heads(ATT_H + 2 * g + 1)
            branch(g, 1)

        pe.wait_ge(exp_done, HEADS)
        pe.wait_ge(probsT_sb, HEADS)
        pe.wait_ge(y_att_sb, ATT_H // 2 + X_H)
        for j in range(4):
            pe.wait_ge(merged_parts, 2 if j < 2 else 4)
            w = parts(N_MIX - 4 + j, 2)
            for k in range(2):
                c = 2 * j + k
                for t in range(TT):
                    for half in range(2):
                        last = product(bank[2 + 2 * t + half][:, :], (merged_high, merged_low), w,
                                       (slice(None), c, slice(t * P, (t + 1) * P)),
                                       (slice(None), k, slice(half * 512, half * 512 + 512)), c == 0, c == KC - 1)
            last.then_inc(pieces_used, 1)

        pe.wait_ge(merged_sb, 12)
        pe.wait_ge(gates_sb, 12)
        for u in range(4):
            pe.wait_ge(h2_sb, u // 2 + 1)
            transposed(h2, u, bank[(6, 7, 0, 1)[u]], h2T_done)
        pe.wait_ge(h2T_sb, 4)
        pe.wait_ge(router_in, 32)
        pe.wait_ge(x2_sb, TT)
        for t in range(TT):
            for c in range(KC):
                last = mm(bank[4][:, t * E:(t + 1) * E], h2T[:, c, t * P:(t + 1) * P], w_rt[:, c, :],
                          start=(c == 0), stop=(c == KC - 1))
        last.then_inc(logits_done, 1)
        pe.wait_ge(mask_sb, 1)
        mm(bank[5][:, 0:E], before, mask[:, 0, :], start=True, stop=True)
        mm(bank[5][:, E:2 * E], ones[:, :], mask[:, 0, :], start=True, stop=False)
        mm(bank[5][:, E:2 * E], before, mask[:, 1, :], start=False, stop=True)
        mm(bank[5][:, 2 * E:3 * E], ones[:, :], mask[:, 0, :], start=True, stop=False)
        mm(bank[5][:, 2 * E:3 * E], ones[:, :], mask[:, 1, :], start=False, stop=True).then_inc(rank_done, 1)
        pe.wait_ge(weights_sb, 1)
        for t in range(TT):
            last = mm(bank[6][0:E, t * P:(t + 1) * P], wexp[:, t, 0:E], ident, start=True, stop=True)
        last.then_inc(wexpT_done, 1)
        pe.wait_ge(wexpT_sb, 1)
        pe.wait_ge(expert_bias_in, 16 * 5)
        for t in range(TT):
            for half in range(2):
                last = mm(acc[t][half][:, :], wexpT[:, t * P:(t + 1) * P], b_down[:, half * 512:half * 512 + 512],
                          start=True, stop=False)
        last.then_inc(acc_open, 1)

        def gather(s):
            pe.wait_ge(gat_ready, s + 1)
            for c in range(KC):
                for t in range(TT):
                    last = mm(tr_ps[:, c * SLOTS:(c + 1) * SLOTS], h2[:, t, c * P:(c + 1) * P], gat[:, t, :],
                              start=(t == 0), stop=(t == TT - 1))
            last.then_inc(gathered, 1)

        def scatter(stop):
            for t in range(TT):
                for half in range(2):
                    last = mm(acc[t][half][:, :], scaT[:, t, :], y_parts[:, half * 512:half * 512 + 512],
                              start=False, stop=stop)
            return last

        gather(0)
        pe.wait_ge(b_parts_ready, 1)
        more = pe.value_load(more_i32[0:1, 0:1], min_val=0, max_val=PASSES - 1)
        with pe.Fori(0, more * (E // 2) + E // 2) as i:
            for u in range(2):
                s = i * 2 + u
                slot0 = 8 if u == 0 else 0
                pe.wait_ge(sel_ready, s + 1)
                pe.wait_ge(up_read, s + 1)
                for k, ps in enumerate((gate_ps, lin_ps)):
                    mm(ps[:, :], sel[:, :], b_parts[:, k * 512:k * 512 + 512], start=True, stop=False)
                pe.wait_ge(xg_sb, s + 1)
                for c in range(KC):
                    pe.wait_ge(piece_in[slot0 + c], i * 16 + 16 * (loads_before(slot0 + c) + 1))
                    for k, ps in enumerate((gate_ps, lin_ps)):
                        for half in range(2):
                            last = mm(ps[64 * half:64 * half + 64, :], xg[:, c, :],
                                      ring[:, slot0 + c, k * F + half * 512:k * F + half * 512 + 512],
                                      start=False, stop=(c == KC - 1))
                    last.then_inc(pieces_used, 1)
                pe.wait_ge(y_ready, s + 1)
                pe.wait_ge(scaT_sb, s + 1)
                scatter(False).then_inc(scattered, 1)
                pe.wait_ge(sca_ready, s + 1)
                for t in range(TT):
                    last = transpose(y_ps[:, t * P:(t + 1) * P], sca[:, t, :], ident)
                last.then_inc(scaT_done, 1)
                pe.wait_ge(hidT_sb, s + 1)
                gather(s + 1)
                pe.wait_ge(hid_ready, s + 1)
                pe.wait_ge(xg_sb, s + 2)
                for c in range(4):
                    last = transpose(tr_ps[:, c * P:(c + 1) * P], hid[:, c * P:(c + 1) * P], ident)
                last.then_inc(hidT_done, 1)
                pe.wait_ge(hidT_sb, s + 2)
                pe.wait_ge(scaT_sb, s + 2)
                pe.wait_ge(w_slot_ready, s + 1)
                for c in range(KC):
                    if c % 2 == 0:
                        pe.wait_ge(down_in[c // 2], (s + 1) * 16)
                    lhsT = hidT[:, (c % 4) * P + 64 * (c // 4):(c % 4) * P + 64 * (c // 4) + 64]
                    for half in range(2):
                        at = (c % 2) * D + half * 512
                        last = mm(y_ps[64 * half:64 * half + 64, :], lhsT, dring[:, c // 2, at:at + 512],
                                  start=(c == 0), stop=(c == KC - 1))
                    if c % 2:
                        last.then_inc(downs_used, 1)
        pe.wait_ge(y_ready, more * E + (E + 1))
        pe.wait_ge(scaT_sb, more * E + (E + 1))
        scatter(True).then_inc(acc_done, 1)



_INS = ["x", "mem", "rel_bias", "norm_mix_g", "w_in", "b_gate", "conv_w", "norm_mem_g", "w_mem_kv",
        "w_br_att", "w_br_conv", "w_br_xatt", "w_out", "norm_ffn_g", "w_router", "b_router",
        "w_gu", "b_gu", "w_down", "b_down", "norm_final_g"]


def kernel(**inputs):
    import numpy as _np
    import concourse.bacc as _bacc
    from concourse import mybir as _mybir
    from concourse.bass_utils import run_bass_kernel_spmd as _run

    nc = _bacc.Bacc("TRN2", target_bir_lowering=False, num_devices=1)
    given = {name: _np.ascontiguousarray(inputs[name]) for name in _INS}
    given["consts"], hot = shape_constants()
    given["rows"] = _np.concatenate([given.pop(k).reshape(-1, P) for k in
                                     ("norm_mix_g", "norm_mem_g", "norm_ffn_g", "b_gate", "conv_w")])
    future = _np.full((1, ATT_H), NEG, _np.float32)
    given["table_hot"] = _np.concatenate([_np.concatenate([given.pop("rel_bias"), future]), hot], axis=1)
    arrays, args = {}, {}
    for name, value in given.items():
        arrays[f"in_{name}_dram"] = value
        args[name] = nc.dram_tensor(f"in_{name}_dram", value.shape, _mybir.dt.from_np(value.dtype), kind="ExternalInput").ap()
    out = nc.dram_tensor("out_0_dram", (1, S, D), _mybir.dt.float32, kind="ExternalOutput").ap()
    scratch = nc.dram_tensor("bias_scratch", [ATT_H, 384], _mybir.dt.float32, kind="Internal").ap()
    trunk_layer(nc, args, out, scratch)
    r = _run(nc, [arrays], core_ids=[0])
    return r.results[0]["out_0_dram"]
```

```python
import concourse.bass as bass
from concourse import mybir
import numpy as np
import math
from contextlib import ExitStack

P = 128
D = 1024
S = 256
M = 256
ATT_H, ATT_D = 8, 64
X_H, X_D = 4, 128
CONV = 512
E = 32
TOPK = 4
BUCKETS = 32
MAX_DIST = 128
EPS = 1e-5
NEG = -1e30
LIMIT = 7.0
ALPHA = 1.702
F = D
KC = D // P
TT = S // P
SLOTS = 64
PASSES = S // SLOTS
STEPS = PASSES * E
TOEP = 3 * P - 1
RING = 16
PIECE = 2048
DRING = 4
IN_ORDER = 4

QA, KA, VA, CB, CC, CU, QX, GL = 0, 512, 1024, 1536, 2048, 2560, 3072, 3584
PROJ = ([("w_mem_kv", 256 * j) for j in range(4)]
        + [("w_in", col + 256 * j) for col in (QA, KA, VA, CC, CU, QX, CB) for j in range(2)])
BRANCHES = [(1, "w_br_conv"), (0, "w_br_att"), (2, "w_br_xatt")]
GROUPS = [(b, w, half) for b, w in BRANCHES for half in range(2)]
N_PROJ = len(PROJ)
FIRST_HEAD = N_PROJ - ATT_H
N_MIX = N_PROJ + 3 * len(GROUPS) + 4
FIRST_CONV = PROJ.index(("w_in", CU))
HEADS = ATT_H + X_H
MIX_RING = 12


def merged_tile(n):
    return GROUPS[n // 2][2] * 4 + (n % 2) * 2


def mixer_slot(p):
    return (p + 8 - (N_MIX - MIX_RING)) % MIX_RING


def mixer_loads(p):
    return sum(mixer_slot(q) == mixer_slot(p) for q in range(p + 1))


def loads_before(slot):
    return sum(mixer_slot(q) == slot for q in range(N_MIX))


C_ID, C_TRI, C_SLOT, C_HALF, C_PICK = 0, P, 2 * P, 3 * P, 4 * P
C_KEPT = C_PICK + STEPS + 1


def shape_constants():
    c = np.zeros((P, C_KEPT + P), np.float32)
    r = np.arange(P)
    c[:, C_ID:C_ID + P] = np.eye(P)
    c[:, C_TRI:C_TRI + P] = np.triu(np.ones((P, P)), 1)
    c[:, C_SLOT:C_SLOT + P] = np.tile(np.arange(SLOTS), 2)[None]
    c[:, C_HALF:C_HALF + P] = (r[:, None] % (2 * E) // E) == (r[None] // SLOTS)
    c[:, C_PICK:C_KEPT] = (r[:, None] % E) == (np.arange(STEPS + 1)[None] % E)
    c[:, C_KEPT:] = np.eye(P)[::-1]
    hot = np.zeros((BUCKETS + 1, TOEP), np.float32)
    exact = BUCKETS // 2
    for i in range(TOEP):
        dist = 2 * P - 1 - i
        if dist < 0:
            hot[BUCKETS, i] = 1.0
        elif dist < exact:
            hot[dist, i] = 1.0
        else:
            large = exact + int(math.log(dist / exact) / math.log(MAX_DIST / exact) * (BUCKETS - exact))
            hot[min(large, BUCKETS - 1), i] = 1.0
    return c, hot


def trunk_layer(nc, a, out, scratch):
    ctx = ExitStack()
    with ctx:
        build(nc, a, out, scratch, ctx)


def build(nc, a, out, scratch, ctx):
    fp32 = mybir.dt.float32
    fp32r = mybir.dt.float32r
    i32 = mybir.dt.int32
    u32 = mybir.dt.uint32
    ALU = mybir.AluOpType
    ACT = mybir.ActivationFunctionType
    AX = mybir.AxisListType

    def sb(name, shape, dt=fp32):
        return nc.alloc_sbuf_tensor(name, shape, dt)

    at_of = {}

    def region(name, shape):
        tensor = sb(name, shape)
        at_of[name] = nc.sbuf_base - 4 * math.prod(shape[1:])
        return tensor

    def rounded(name, shape, where, at):
        return nc.alloc_sbuf_tensor_at(name, shape, fp32r, offset=at_of[where] + 4 * at)

    ring = region("ring", [P, RING, PIECE])
    dring = region("dring", [P, DRING, PIECE])
    region_x = region("region_x", [P, 2048])
    region_h = region("region_h", [P, 2048])
    region_r = region("region_r", [P, 6152])

    scaT = rounded("scaT", [P, TT, P], "region_r", 5000)
    sel = rounded("sel", [P, P], "region_r", 5256)
    b_parts = rounded("b_parts", [P, 1024], "region_r", 2048)
    y_parts = sb("y_parts", [P, 1024], fp32r)
    consts = sb("consts", [P, C_KEPT])
    counting = sb("counting", [P, 2, P], mybir.dt.bfloat16)
    mask = nc.alloc_sbuf_tensor_at("mask", [P, TT, E], mybir.dt.bfloat16,
                                   offset=at_of["region_r"] + 4 * 5384)
    cols = sb("cols", [P, 60])
    zero = sb("zero", [P, 2])
    stats = sb("stats", [P, 3, HEADS, 2])
    norm = sb("norm", [P, 4, 8])
    more_i32 = sb("more_i32", [1, 1], i32)
    best_u = sb("best_u", [P, TT, 8], u32)

    ident = consts[:, C_ID:C_ID + P]
    before = consts[:, C_TRI:C_TRI + P]
    slot_no = consts[:, C_SLOT:C_SLOT + P]
    half_of = consts[:, C_HALF:C_HALF + P]
    pick = consts[:, C_PICK:C_KEPT]
    g_mix, g_mem, g_ffn = cols[:, 0:8], cols[:, 8:16], cols[:, 16:24]
    b_gate = cols[:, 24:48]
    conv_w = cols[:, 48:60]
    top, negtop, sums = stats[:, 0], stats[:, 1], stats[:, 2]

    w_high = [rounded(f"w_high{n}", [P, PIECE], "ring", (13 + n) * PIECE) for n in range(3)]
    w_low = [rounded(f"w_low{n}", [P, PIECE], "ring", n * PIECE) for n in range(MIX_RING)]
    hT = dring[:, 0, :].rearrange("p (c t) -> p c t", c=KC)
    hT_low = rounded("hT_low", [P, KC, S], "dring", 0)
    hT_high = rounded("hT_high", [P, KC, S], "dring", PIECE)
    memT = dring[:, 2, :].rearrange("p (c t) -> p c t", c=KC)
    memT_low = rounded("memT_low", [P, KC, M], "dring", 2 * PIECE)
    memT_high = rounded("memT_high", [P, KC, M], "dring", 3 * PIECE)
    qk = dring[:, 2, :].rearrange("p (c t) -> p c t", c=8)
    y_att_high = rounded("y_att_high", [P, 4, S], "dring", 2 * PIECE)
    y_att_low = rounded("y_att_low", [P, 4, S], "dring", 2 * PIECE + 1024)
    merged = dring[:, 3, :].rearrange("p (c t) -> p c t", c=KC)
    merged_low = rounded("merged_low", [P, KC, S], "dring", 3 * PIECE)
    merged_high = rounded("merged_high", [P, KC, S], "region_r", 0)
    mem_nat = region_x[:, :].rearrange("p (t d) -> p t d", t=TT)
    qx = region_x[:, 0:1024].rearrange("p (c t) -> p c t", c=X_H)
    kx = region_x[:, 1024:2048].rearrange("p (c t) -> p c t", c=X_H)
    y_x_high = rounded("y_x_high", [P, X_H, S], "region_x", 0)
    y_x_low = rounded("y_x_low", [P, X_H, S], "region_x", 1024)
    x2 = mem_nat
    x_nat = region_h[:, :].rearrange("p (t d) -> p t d", t=TT)
    probs = [region_h[:, 512 * n:512 * n + 512] for n in range(2)]
    probsT = [region_h[:, 1024 + 512 * n:1024 + 512 * n + 512] for n in range(2)]
    x_again = x_nat
    h2 = x_nat
    squares = ring[:, 14, :].rearrange("p (t d) -> p t d", t=TT)
    bias = region_r[:, 0:2048].rearrange("p (h k) -> p h k", h=ATT_H)
    v_att = region_r[:, 2048:3072].rearrange("p (t c) -> p t c", t=TT)
    y_conv = region_r[:, 3072:4096].rearrange("p (c t) -> p c t", c=4)
    y_conv_low = rounded("y_conv_low", [P, 4, S], "region_r", 3072)
    y_conv_high = rounded("y_conv_high", [P, 4, S], "ring", 12 * PIECE)
    z = region_r[:, 4096:4096 + 4 * (S + 2)].rearrange("p (c t) -> p c t", c=4)
    vx = ring[:, 12, 1024:2048].rearrange("p (t c) -> p t c", t=TT)
    flip = region_r[:, 3072:3072 + P]
    sig = [region_r[:, 5128 + 512 * n:5640 + 512 * n] for n in range(2)]
    rows = region_r[0:60, 5128:5256]
    table_hot = region_r[0:BUCKETS + 1, 5256:5264 + TOEP]
    table, hot = table_hot[:, 0:ATT_H], table_hot[:, ATT_H:]
    bias_of_dist = region_r[0:ATT_H, 5650:5650 + TOEP]
    squares2 = region_r[:, 3072:4096].unsqueeze(1).broadcast_to([P, TT, D])

    b_gu = region_r[:, 4096:5120]
    b_down = ring[0:E, 9, 0:D]
    xg = region_r[:, 0:512].rearrange("p (c s) -> p c s", c=KC)
    g_sb = region_r[:, 512:1024]
    sg = region_r[:, 1024:1536]
    hid = region_r[:, 1536:2048]
    hidT = region_r[:, 3072:3584]
    x2T = region_r[:, 0:2048].rearrange("p (c t) -> p c t", c=KC)
    logit_parts = region_r[:, 4096:4352]
    place = region_r[:, 4096:4096 + 2 * (STEPS + 1)].rearrange("p (t s) -> p t s", t=TT)
    wexp = region_r[:, 4354:4354 + 2 * (STEPS + 1)].rearrange("p (t s) -> p t s", t=TT)
    gat = region_r[:, 4612:4612 + TT * SLOTS].rearrange("p (t s) -> p t s", t=TT)
    sca = region_r[:, 4740:4740 + TT * P].rearrange("p (t s) -> p t s", t=TT)
    w_slot = region_r[:, 6132:6133]
    unused = region_r[:, 3584:3584 + TT * P]
    logit = region_r[:, 5316:5380].rearrange("p (t e) -> p t e", t=TT)
    best = region_r[:, 5476:5492].rearrange("p (t k) -> p t k", t=TT)
    best_i = region_r[:, 5492:5508].rearrange("p (t k) -> p t k", t=TT)
    elog = region_r[:, 5876:5940].rearrange("p (t e) -> p t e", t=TT)
    gain_out = ring[:, 8, 0:D]
    rank = region_r[:, 5508:5572].rearrange("p (t e) -> p t e", t=TT)
    small = region_r[:, 5572:5588]
    w_rt = region_r[:, 5588:5844].rearrange("p (c e) -> p c e", c=KC)
    b_rt = region_r[:, 5844:5876]
    wexpT = region_r[0:E, 5876:6132]

    bank = [nc.alloc_psum_tensor(f"bank{n}", [P, 512], fp32) for n in range(8)]
    acc = [bank[0:2], bank[2:4]]
    gate_ps, lin_ps, tr_ps, y_ps = bank[4], bank[5], bank[6], bank[7]

    def sem(name):
        return ctx.enter_context(nc.semaphore(name))

    x_in = [sem(f"x_in{t}") for t in range(TT)]
    mem_in = [sem(f"mem_in{t}") for t in range(TT)]
    table_in, flip_in, rows_in, bias_in, scratch_out = sem("table_in"), sem("flip_in"), sem("rows_in"), sem("bias_in"), sem("scratch_out")
    x_again_in, b_gu_in, b_down_in, router_in = sem("x_again_in"), sem("b_gu_in"), sem("b_down_in"), sem("router_in")
    final_gain_in, out_done = sem("final_gain_in"), sem("out_done")
    piece_in = [sem(f"piece_in{n}") for n in range(RING)]
    down_in = [sem(f"down_in{n}") for n in range(DRING)]
    pieces_used, downs_used = sem("pieces_used"), sem("downs_used")
    cols_done, dist_done, bias_flipped = sem("cols_done"), sem("dist_done"), sem("bias_flipped")
    hT_done, scores_done = sem("hT_done"), sem("scores_done")
    probsT_done, pv_done, branch_done = sem("probsT_done"), sem("pv_done"), sem("branch_done")
    mixed_done = sem("mixed_done")
    x2T_done, logit_parts_done, logits_done, rank_done = sem("x2T_done"), sem("logit_parts_done"), sem("logits_done"), sem("rank_done")
    wexpT_done, acc_done = sem("wexpT_done"), sem("acc_done")
    gathered, scaT_done, hidT_done, scattered = sem("gathered"), sem("scaT_done"), sem("hidT_done"), sem("scattered")
    w_high_ready, w_low_ready = sem("w_high_ready"), sem("w_low_ready")
    gained, act_high, hT_parts = sem("gained"), sem("act_high"), sem("hT_parts")
    conv_high, conv_parts, y_att_high_ready = sem("conv_high"), sem("conv_parts"), sem("y_att_high_ready")
    merged_high_ready, merged_parts = sem("merged_high_ready"), sem("merged_parts")
    cols_sb, dist_sb, mean_done, normed = sem("cols_sb"), sem("dist_sb"), sem("mean_done"), sem("normed")
    bias_sb = sem("bias_sb")
    proj_sb, att_scores_read, top_ready = sem("proj_sb"), sem("att_scores_read"), sem("top_ready")
    probs_ready, merged_sb, x2_sb, h2_sb = sem("probs_ready"), sem("merged_sb"), sem("x2_sb"), sem("h2_sb")
    x2T_sb, logit_parts_sb, w_rt_ready, counting_ready = sem("x2T_sb"), sem("logit_parts_sb"), sem("w_rt_ready"), sem("counting_ready")
    best_ready, mask_sb, weights_sb, wexpT_sb = sem("best_ready"), sem("mask_sb"), sem("weights_sb"), sem("wexpT_sb")
    passes_ready = sem("passes_ready")
    gat_ready, sca_ready, sel_ready, xg_sb = sem("gat_ready"), sem("sca_ready"), sem("sel_ready"), sem("xg_sb")
    g_ready, up_read, hid_half, hid_ready = sem("g_ready"), sem("up_read"), sem("hid_half"), sem("hid_ready")
    scaT_sb, y_ready = sem("scaT_sb"), sem("y_ready")
    fin_sb, dve_step = sem("fin_sb"), sem("dve_step")
    x2T_copied = sem("x2T_copied")
    sq_done, root_done, exp_done, probsT_sb = sem("sq_done"), sem("root_done"), sem("exp_done"), sem("probsT_sb")
    y_att_sb, gates_sb, router_exp = sem("y_att_sb"), sem("gates_sb"), sem("router_exp")
    sig_ready, hidT_sb, w_slot_ready, y_high = sem("sig_ready"), sem("hidT_sb"), sem("w_slot_ready"), sem("y_high")

    block = ctx.enter_context(nc.Block())

    @block.sync
    def _(sp):
        def mixer_piece(p, src, chunks):
            if p >= MIX_RING:
                sp.wait_ge(pieces_used, p - MIX_RING + 1)
            q = mixer_slot(p)
            sp.dma_start(ring[:, q, :].rearrange("p (c n) -> p c n", c=chunks), src).then_inc(piece_in[q], 16)

        sp.dma_start(table_hot, a["table_hot"]).then_inc(table_in, 16)
        for t in range(TT):
            sp.dma_start(mem_nat[:, t, :], a["mem"][0, t * P:(t + 1) * P, :]).then_inc(mem_in[t], 16)
        sp.dma_start(rows, a["rows"]).then_inc(rows_in, 16)
        sp.dma_start(consts[:, :], a["consts"][:, 0:C_KEPT]).then_inc(rows_in, 16)
        p = 0
        for name, col in PROJ:
            if p == 1:
                for t in range(TT):
                    sp.dma_start(x_nat[:, t, :], a["x"][0, t * P:(t + 1) * P, :]).then_inc(x_in[t], 16)
                sp.dma_start(flip, a["consts"][:, C_KEPT:]).then_inc(flip_in, 16)
            if p == 4:
                sp.wait_ge(bias_in, 16)
            mixer_piece(p, a[name][0, :, col:col + 256].rearrange("(c p) n -> p c n", p=P), KC)
            p += 1
        for b, name, half in GROUPS:
            for j in range(2):
                col = GL + b * D + half * 512 + j * 256
                mixer_piece(p, a["w_in"][0, :, col:col + 256].rearrange("(c p) n -> p c n", p=P), KC)
                p += 1
            mixer_piece(p, a[name][0, :, half * 512:half * 512 + 512].rearrange("(c p) n -> p c n", p=P), 4)
            p += 1
        for j in range(4):
            mixer_piece(p, a["w_out"][0, j * 256:(j + 1) * 256, :].rearrange("(c p) n -> p c n", p=P), 2)
            p += 1
        sp.wait_ge(y_att_sb, ATT_H // 2 + X_H)
        sp.dma_start(x_again, a["x"][0].rearrange("(t p) d -> p t d", p=P)).then_inc(x_again_in, 16)

        def up_piece(expert, slot, c):
            sp.dma_start(ring[:, slot, :], a["w_gu"][0, bass.ds(expert, 1), c * P:(c + 1) * P, :]
                         .rearrange("e p n -> (e p) n")).then_inc(piece_in[slot], 16)

        def expert_up(expert, slot0, uses):
            for c in range(KC):
                sp.wait_ge(pieces_used, uses + c)
                up_piece(expert, slot0 + c, c)

        def down_piece(expert, j):
            sp.dma_start(dring[:, j, :].rearrange("p (c n) -> p c n", c=2),
                         a["w_down"][0, bass.ds(expert, 1), j * 256:(j + 1) * 256, :]
                         .rearrange("e (c p) n -> p (e c) n", p=P)).then_inc(down_in[j], 16)

        def expert_down(expert, uses):
            for j in range(DRING):
                sp.wait_ge(downs_used, uses + j)
                down_piece(expert, j)

        for n in range(MIX_RING):
            used = N_MIX - MIX_RING + 1 + n
            sp.wait_ge(pieces_used, used)
            if n < MIX_RING - 8:
                up_piece(0, 8 + n, n)
            else:
                up_piece(1, n - (MIX_RING - 8), n - (MIX_RING - 8))
            if used == N_PROJ + 11:
                up_piece(0, 12, 4)
            if used == N_PROJ + 12:
                down_piece(0, 2)
            if used == N_PROJ + 17:
                down_piece(0, 0)
                down_piece(0, 1)
            if used > N_MIX - 3:
                up_piece(0, 13 + (used - 1) % 3, 5 + (used - 1) % 3)
        down_piece(0, 3)
        sp.wait_ge(passes_ready, 1)
        more = sp.value_load(more_i32[0:1, 0:1], min_val=0, max_val=PASSES - 1)
        with sp.Fori(0, more * (E // 2) + (E // 2 - 1 - IN_ORDER)) as i:
            expert_up((i * 2 + 2) % E, 8, i * 16 + (N_MIX - RING + 17))
            expert_down((i * 2 + 1) % E, i * 8 + 1)
            expert_up((i * 2 + 3) % E, 0, i * 16 + (N_MIX - RING + 25))
            expert_down((i * 2 + 2) % E, i * 8 + 5)
        ups, downs = more * (KC * E) + (N_MIX - RING + 1), more * (DRING * E) + (1 - DRING)
        e0 = E - 2 * IN_ORDER
        expert_down(e0 - 1, downs + DRING * (e0 - 1))
        with sp.Fori(0, IN_ORDER) as i:
            for u in range(2):
                e = i * 2 + (e0 + u)
                expert_up(e, 8 * (1 - u), ups + e * KC)
                expert_down(e, downs + e * DRING)
        sp.wait_ge(pieces_used, more * (KC * E) + (KC * (E - 1) + N_MIX))
        sp.dma_start(b_down, a["b_down"][0]).then_inc(b_down_in, 16)
        sp.dma_start(gain_out, a["norm_final_g"].unsqueeze(0).broadcast_to([P, D])).then_inc(final_gain_in, 16)
        for t in range(TT):
            sp.wait_ge(fin_sb, t + 1)
            sp.dma_start(out[0, t * P:(t + 1) * P, :], x2[:, t, :]).then_inc(out_done, 16)
        sp.wait_ge(out_done, 16 * TT)

    @block.gpsimd
    def _(pool):
        pool.wait_ge(w_high_ready, 1)
        pool.tensor_tensor(w_low[mixer_slot(0)][:, :], ring[:, mixer_slot(0), :], w_high[0][:, :].bitcast(fp32), ALU.subtract)\
            .then_inc(w_low_ready, 1)
        pool.wait_ge(dist_sb, 1)
        pool.dma_start(scratch[:, 0:TOEP], bias_of_dist).then_inc(scratch_out, 16)
        pool.wait_ge(scratch_out, 16)
        pool.dma_start(bias, bass.AP(scratch.tensor, 0, [[1, P], [384, ATT_H], [1, 2 * P]])).then_inc(bias_in, 16)
        pool.wait_ge(conv_parts, 2)
        pool.dma_start(b_gu, a["b_gu"]).then_inc(b_gu_in, 16)
        pool.wait_ge(merged_sb, 2 * len(GROUPS))
        pool.dma_start(w_rt, a["w_router"][0].rearrange("(c p) e -> p c e", p=P)).then_inc(router_in, 16)
        pool.dma_start(b_rt, a["b_router"].broadcast_to([P, E])).then_inc(router_in, 16)

    @block.scalar
    def _(act):
        act.wait_ge(mean_done, 1)
        act.activation(norm[:, 0, 4:6], norm[:, 0, 2:4], ACT.Sqrt)

        def square_sums(src, into, n, t):
            act.activation(into[:, t, :], src[:, t, :], ACT.Square, accum_out=norm[:, n, t:t + 1]).then_inc(sq_done, 1)

        def root(n):
            act.wait_ge(mean_done, n + 2)
            act.activation(norm[:, n, 4:6], norm[:, n, 2:4], ACT.Sqrt).then_inc(root_done, 1)

        def w_high_part(p):
            if p >= N_MIX:
                return
            q = mixer_slot(p)
            act.wait_ge(piece_in[q], 16 * mixer_loads(p))
            if p >= 3:
                act.wait_ge(pieces_used, p - 2)
            act.activation(w_high[p % 3][:, :], ring[:, q, :], ACT.Copy).then_inc(w_high_ready, 1)

        def act_high_part(u, src, dst):
            act.wait_ge(gained, u + 1)
            t, half = u % 4 // 2, u % 2
            cut = (slice(None), slice(4 * half, 4 * half + 4), slice(t * P, (t + 1) * P))
            act.activation(dst[cut], src[cut], ACT.Copy).then_inc(act_high, 1)

        for t in range(TT):
            act.wait_ge(mem_in[t], 16)
            square_sums(mem_nat, squares, 0, t)
        root(0)
        w_high_part(0)
        for u in range(4):
            act_high_part(u, memT, memT_high)
        act.wait_ge(sq_done, TT)
        for t in range(TT):
            act.wait_ge(x_in[t], 16)
            square_sums(x_nat, squares, 1, t)
        act.wait_ge(sq_done, 2 * TT)
        root(1)
        w_high_part(1)
        w_high_part(2)

        def exp(hh):
            act.wait_ge(top_ready, hh + 1)
            pr = probs[hh % 2]
            if hh < ATT_H:
                for n, cut in enumerate((slice(0, 256), slice(256, 384))):
                    last = act.activation(pr[:, cut], pr[:, cut], ACT.Exp, bias=negtop[:, hh, n:n + 1],
                                          accum_out=sums[:, hh, n:n + 1])
            else:
                act.wait_ge(probsT_done, hh - 1)
                for n in range(TT):
                    cut = slice(n * 256, n * 256 + 256)
                    last = act.activation(pr[:, cut], bank[2 + hh % 2][:, cut], ACT.Exp,
                                          bias=negtop[:, hh, n:n + 1], scale=X_D ** -0.5,
                                          accum_out=sums[:, hh, n:n + 1])
            last.then_inc(exp_done, 1)

        def probsT_copy(hh):
            act.wait_ge(probsT_done, hh + 1)
            n = 384 if hh < ATT_H else 512
            act.activation(probsT[hh % 2][:, 0:n], bank[4][:, 0:n], ACT.Copy).then_inc(probsT_sb, 1)

        def pv_high(hh):
            if hh < ATT_H and hh % 2 == 0:
                return
            u, dst = ((hh // 2, y_att_high[:, hh // 2, :]) if hh < ATT_H else
                      (hh - ATT_H // 2, y_x_high[:, hh - ATT_H, :]))
            act.wait_ge(pv_done, u + 1)
            act.activation(dst, bank[5][:, 0:256], ACT.Copy).then_inc(y_att_high_ready, 1)

        def heads(j):
            if 0 <= j - 2 < HEADS:
                probsT_copy(j - 2)
            if 0 <= j - 3 < HEADS:
                pv_high(j - 3)
            if 0 <= j < HEADS:
                exp(j)

        for p in range(N_PROJ):
            if p == 0:
                for u in range(4):
                    act_high_part(4 + u, hT, hT_high)
            w_high_part(p + 3)
            if PROJ[p][0] == "w_in" and CB <= PROJ[p][1] < CC:
                k = (PROJ[p][1] - CB) // P
                act.wait_ge(proj_sb, p + 1)
                act.activation(y_conv_high[:, k:k + 2, :], y_conv[:, k:k + 2, :], ACT.Copy).then_inc(conv_high, 1)
            heads(p - FIRST_HEAD)

        def sigmoid(n):
            b, _, half = GROUPS[n // 2]
            act.wait_ge(pieces_used, N_PROJ + 3 * (n // 2) + n % 2 + 1)
            if n >= 2:
                act.wait_ge(merged_sb, n - 1)
            for k in range(2):
                tile = b * 8 + half * 4 + (n % 2) * 2 + k
                last = act.activation(sig[n % 2][:, k * 256:k * 256 + 256], bank[n % 2][:, k * 256:k * 256 + 256],
                                      ACT.Sigmoid, bias=b_gate[:, tile:tile + 1])
            last.then_inc(gates_sb, 1)

        def merged_high_part(n):
            if n < 8:
                return
            tile = merged_tile(n)
            act.wait_ge(merged_sb, n + 1)
            act.activation(merged_high[:, tile:tile + 2, :], merged[:, tile:tile + 2, :], ACT.Copy)\
                .then_inc(merged_high_ready, 1)

        for g in range(len(GROUPS)):
            p = N_PROJ + 3 * g
            sigmoid(2 * g)
            w_high_part(p + 3)
            heads(ATT_H + 2 * g)
            sigmoid(2 * g + 1)
            w_high_part(p + 4)
            heads(ATT_H + 2 * g + 1)
            merged_high_part(2 * g)
            w_high_part(p + 5)
            merged_high_part(2 * g + 1)
        w_high_part(N_MIX - 1)

        act.wait_ge(root_done, 2)
        act.activation(norm[:, 2, 4:6], norm[:, 1, 2:4], ACT.Sqrt)
        for u in range(2):
            act.wait_ge(x2T_done, u + 1)
            act.activation(x2T[:, 4 * u:4 * u + 4, 0:P], bank[6 + u][:, :].rearrange("p (c t) -> p c t", c=4), ACT.Copy)\
                .then_inc(x2T_copied, 1)
        for t in range(TT):
            act.wait_ge(x2_sb, 2 * t + 2)
            act.wait_ge(sq_done, 2 * TT + t)
            square_sums(x2, squares2, 2, t)
        root(2)
        act.wait_ge(best_ready, 1)
        for t in range(TT):
            last = act.activation(elog[:, t, :], logit[:, t, :], ACT.Exp, bias=small[:, t:t + 1])
        last.then_inc(router_exp, 1)
        for t in range(TT):
            act.activation(h2[:, t, :], x2[:, t, :], ACT.Copy, scale=norm[:, 2, 6 + t:7 + t]).then_inc(h2_sb, 1)
        act.wait_ge(wexpT_done, 1)
        act.activation(wexpT, bank[7][0:E, 0:TT * P], ACT.Copy).then_inc(wexpT_sb, 1)

        act.wait_ge(passes_ready, 1)
        more = act.value_load(more_i32[0:1, 0:1], min_val=0, max_val=PASSES - 1)
        with act.Fori(0, more * (E // 2) + E // 2) as i:
            for u in range(2):
                s = i * 2 + u
                act.wait_ge(g_ready, s + 1)
                act.activation(sg, g_sb, ACT.Sigmoid, scale=ALPHA).then_inc(sig_ready, 1)
                act.wait_ge(scaT_done, s + 1)
                act.wait_ge(y_ready, s + 1)
                act.activation(unused, y_ps[:, 0:TT * P], ACT.Copy, accum_out=w_slot).then_inc(w_slot_ready, 1)
                act.wait_ge(hidT_done, s + 1)
                act.activation(hidT, tr_ps[:, :], ACT.Copy).then_inc(hidT_sb, 1)
                act.wait_ge(downs_used, (s + 1) * DRING)
                act.wait_ge(w_slot_ready, s + 1)
                act.activation(y_parts[0:64, 0:512], y_ps[0:64, :], ACT.Copy, scale=w_slot[0:64, :])
                act.activation(y_parts[64:128, 512:1024], y_ps[64:128, :], ACT.Copy, scale=w_slot[64:128, :])\
                    .then_inc(y_high, 1)

        act.activation(norm[:, 3, 4:6], norm[:, 1, 2:4], ACT.Sqrt)
        for t in range(TT):
            act.wait_ge(acc_done, t + 1)
            for half in range(2):
                last = act.activation(h2[:, t, half * 512:half * 512 + 512], acc[t][half][:, :], ACT.Square,
                                      accum_out=norm[:, 3, 2 * t + half:2 * t + half + 1])
            last.then_inc(sq_done, 1)
            act.wait_ge(mean_done, 5 + t)
            act.activation(norm[:, 3, 6 + t:7 + t], norm[:, 3, 4 + t:5 + t], ACT.Sqrt).then_inc(root_done, 1)

    @block.vector
    def _(dve):
        steps = [0]

        def link(ins):
            steps[0] += 1
            ins.then_inc(dve_step, 1)
            dve.wait_ge(dve_step, steps[0])

        dve.memset(norm[:, 0, 2:4], 1.0).then_inc(mean_done, 1)
        dve.memset(counting[:, 1, :], 1.0)
        dve.memset(z[:, :, 0:2], 0.0)

        def rstd(n):
            dve.wait_ge(sq_done, TT * (n + 1))
            dve.tensor_scalar(norm[:, n, 2:4], norm[:, n, 0:2], 1.0 / D, EPS, ALU.mult, ALU.add).then_inc(mean_done, 1)
            dve.wait_ge(root_done, n + 1)
            link(dve.reciprocal(norm[:, n, 6:8], norm[:, n, 4:6]))

        def normalise(n, src, dst, done):
            for t in range(TT):
                dve.tensor_scalar(dst[:, t, :], src[:, t, :], norm[:, n, 6 + t:7 + t], None, ALU.mult).then_inc(done, 1)

        def with_gain(ps, gain, dst, half, t, done):
            g4 = gain[:, 4 * half:4 * half + 4].unsqueeze(2).broadcast_to([P, 4, P])
            dve.tensor_tensor(dst[:, 4 * half:4 * half + 4, t * P:(t + 1) * P],
                              ps[:, :].rearrange("p (c t) -> p c t", c=4), g4, ALU.mult).then_inc(done, 1)

        dve.wait_ge(dist_done, 1)
        dve.tensor_copy(bias_of_dist, bank[3][0:ATT_H, 0:TOEP]).then_inc(dist_sb, 1)
        dve.wait_ge(cols_done, 1)
        dve.tensor_copy(cols[:, :], bank[2][:, 0:60]).then_inc(cols_sb, 1)
        def act_low_parts(u0, src, high, low):
            for u in range(u0, u0 + 4):
                dve.wait_ge(act_high, u + 1)
                t, half = u % 4 // 2, u % 2
                cut = (slice(None), slice(4 * half, 4 * half + 4), slice(t * P, (t + 1) * P))
                dve.tensor_tensor(low[cut], src[cut], high[cut].bitcast(fp32), ALU.subtract).then_inc(hT_parts, 1)

        def w_low_part(p):
            if p >= N_MIX:
                return
            q = mixer_slot(p)
            if p == 1:
                dve.wait_ge(w_low_ready, 1)
            dve.wait_ge(w_high_ready, p + 1)
            dve.tensor_tensor(w_low[q][:, :], ring[:, q, :], w_high[p % 3][:, :].bitcast(fp32), ALU.subtract)\
                .then_inc(w_low_ready, 1)

        rstd(0)
        normalise(0, mem_nat, mem_nat, normed)
        dve.wait_ge(cols_sb, 1)
        for u in range(4):
            dve.wait_ge(hT_done, u + 1)
            with_gain(bank[4 + u], g_mem, memT, u % 2, u // 2, gained)
        act_low_parts(0, memT, memT_high, memT_low)
        rstd(1)
        normalise(1, x_nat, x_nat, normed)
        w_low_part(1)
        w_low_part(2)

        def projection(u):
            dve.wait_ge(pieces_used, u + 1)
            ps = bank[u % 2][:, :].rearrange("p (k t) -> p k t", k=2)
            name, col = PROJ[u]
            if name == "w_mem_kv":
                j = col // 256
                ins = (dve.tensor_copy(kx[:, 2 * j:2 * j + 2, :], ps) if j < 2 else
                       dve.tensor_copy(vx[:, :, (j - 2) * 256:(j - 1) * 256], ps))
            elif col < VA:
                ins = dve.tensor_copy(qk[:, col // P:col // P + 2, :], ps)
            elif col < CB:
                ins = dve.tensor_copy(v_att[:, :, col - VA:col - VA + 256], ps)
            elif col >= QX:
                ins = dve.tensor_copy(qx[:, (col - QX) // P:(col - QX) // P + 2, :], ps)
            elif col >= CU:
                k = (col - CU) // P
                dve.wait_ge(proj_sb, u - 1)
                ins = dve.tensor_tensor(z[:, k:k + 2, 2:], ps, z[:, k:k + 2, 2:], ALU.mult)
            elif col >= CC:
                k = (col - CC) // P
                ins = dve.tensor_copy(z[:, k:k + 2, 2:], ps)
            else:
                k = (col - CB) // P
                ins = dve.tensor_tensor(y_conv[:, k:k + 2, :], ps, y_conv[:, k:k + 2, :], ALU.mult)
            ins.then_inc(proj_sb, 1)
            if name == "w_in" and col >= CU:
                dve.wait_ge(proj_sb, u + 1)
                c = u - FIRST_CONV
                link(dve.tensor_scalar(y_conv[:, c, :], z[:, c, 0:S], conv_w[:, c:c + 1], None, ALU.mult))
                for tap in (1, 2):
                    w = conv_w[:, 4 * tap + c:4 * tap + c + 1]
                    link(dve.scalar_tensor_tensor(y_conv[:, c, :], z[:, c, tap:tap + S], w, y_conv[:, c, :],
                                                  ALU.mult, ALU.add))

        def head_top(hh):
            dve.wait_ge(scores_done, hh + 1)
            ps, pr = bank[2 + hh % 2], probs[hh % 2]
            if hh < ATT_H:
                if hh == 0:
                    dve.wait_ge(bias_sb, 4)
                if hh >= 2:
                    dve.wait_ge(probsT_done, hh - 1)
                dve.scalar_tensor_tensor(pr[:, 0:256], ps[:, 0:256], ATT_D ** -0.5, bias[:, hh, :], ALU.mult, ALU.add)
                dve.scalar_tensor_tensor(pr[:, 256:384], ps[:, 256:384], ATT_D ** -0.5, bias[:, hh, 128:256],
                                         ALU.mult, ALU.add).then_inc(att_scores_read, 1)
                dve.wait_ge(att_scores_read, hh + 1)
                dve.tensor_reduce(top[:, hh, 0:1], pr[:, 0:256], AX.X, ALU.max)
                link(dve.tensor_reduce(top[:, hh, 1:2], pr[:, 256:384], AX.X, ALU.max))
                scale = 1.0
            else:
                link(dve.tensor_reduce(top[:, hh, :], ps[:, :].rearrange("p (t k) -> p t k", t=TT), AX.X, ALU.max))
                scale = X_D ** -0.5
            dve.tensor_scalar(negtop[:, hh, :], top[:, hh, :], -scale, None, ALU.mult).then_inc(top_ready, 1)

        def head_norm(hh):
            dve.wait_ge(exp_done, hh + 1)
            link(dve.reciprocal(top[:, hh, :], sums[:, hh, :]))
            pr = probs[hh % 2]
            cuts = (slice(0, 256), slice(256, 384 if hh < ATT_H else 512))
            for n, cut in enumerate(cuts):
                last = dve.tensor_scalar(pr[:, cut], pr[:, cut], top[:, hh, n:n + 1], None, ALU.mult)
            last.then_inc(probs_ready, 1)

        def pv_low(hh):
            if hh < ATT_H and hh % 2 == 0:
                return
            u = hh // 2 if hh < ATT_H else hh - ATT_H // 2
            high, low, k = (y_att_high, y_att_low, hh // 2) if hh < ATT_H else (y_x_high, y_x_low, hh - ATT_H)
            dve.wait_ge(y_att_high_ready, u + 1)
            dve.tensor_tensor(low[:, k, :], bank[5][:, 0:256], high[:, k, :].bitcast(fp32), ALU.subtract)\
                .then_inc(y_att_sb, 1)

        def heads_before(j):
            if 0 <= j - 4 < HEADS:
                pv_low(j - 4)
            if 0 <= j - 1 < HEADS:
                head_norm(j - 1)

        def conv_low(k):
            dve.wait_ge(conv_high, k // 2 + 1)
            dve.tensor_tensor(y_conv_low[:, k:k + 2, :], y_conv[:, k:k + 2, :],
                              y_conv_high[:, k:k + 2, :].bitcast(fp32), ALU.subtract).then_inc(conv_parts, 1)

        for p in range(N_PROJ):
            heads_before(p - FIRST_HEAD)
            projection(p)
            if p >= FIRST_HEAD:
                head_top(p - FIRST_HEAD)
            if p == 0:
                for u in range(4):
                    dve.wait_ge(hT_done, 4 + u + 1)
                    with_gain(bank[4 + u], g_mix, hT, u % 2, u // 2, gained)
                act_low_parts(4, hT, hT_high, hT_low)
            w_low_part(p + 3)
            if p in (3, 4):
                for j in range(2 * (p - 3), 2 * (p - 2)):
                    dve.wait_ge(bias_flipped, j + 1)
                    dve.tensor_copy(bias[:, 2 * j:2 * j + 2, :], bank[2 + j % 2][:, :].rearrange("p (h k) -> p h k", h=2))\
                        .then_inc(bias_sb, 1)
            if p == N_PROJ - 1:
                conv_low(0)

        def combine(n):
            g = n // 2
            tile = merged_tile(n)
            dst = merged[:, tile:tile + 2, :].rearrange("p c t -> p (c t)")
            dve.wait_ge(gates_sb, n + 1)
            if n % 2:
                dve.wait_ge(pieces_used, N_PROJ + 3 * g + 3)
            else:
                dve.wait_ge(branch_done, g + 1)
            if g < 2:
                dve.tensor_tensor(dst, bank[6 + n % 2][:, :], sig[n % 2], ALU.mult).then_inc(merged_sb, 1)
            else:
                link(dve.tensor_tensor(sig[n % 2], bank[6 + n % 2][:, :], sig[n % 2], ALU.mult))
                dve.wait_ge(merged_sb, n)
                dve.tensor_tensor(dst, dst, sig[n % 2], ALU.add).then_inc(merged_sb, 1)

        def merged_low_part(n):
            if n < 8:
                return
            tile = merged_tile(n)
            dve.wait_ge(merged_high_ready, n - 7)
            dve.tensor_tensor(merged_low[:, tile:tile + 2, :], merged[:, tile:tile + 2, :],
                              merged_high[:, tile:tile + 2, :].bitcast(fp32), ALU.subtract).then_inc(merged_parts, 1)

        heads_before(ATT_H)
        for g in range(len(GROUPS)):
            p = N_PROJ + 3 * g
            for u in range(2):
                j = ATT_H + 2 * g + u
                if j < HEADS:
                    head_top(j)
                if u == 0:
                    w_low_part(p + 3)
                heads_before(j + 1)
                if u == 0:
                    if g == 0:
                        conv_low(2)
                    w_low_part(p + 4)
                    combine(2 * g)
            merged_low_part(2 * g)
            combine(2 * g + 1)
            w_low_part(p + 5)
            merged_low_part(2 * g + 1)
        w_low_part(N_MIX - 1)

        dve.wait_ge(b_gu_in, 16)
        dve.tensor_copy(b_parts[0:64, :], b_gu[0:64, :])
        link(dve.tensor_copy(y_parts[64:128, :], b_gu[64:128, :]))
        link(dve.tensor_tensor(b_parts[64:128, :], b_gu[64:128, :], y_parts[64:128, :].bitcast(fp32), ALU.subtract))
        dve.wait_ge(router_in, 32)
        dve.tensor_tensor(w_rt, w_rt, g_ffn.unsqueeze(2).broadcast_to([P, KC, E]), ALU.mult).then_inc(w_rt_ready, 1)
        dve.tensor_copy(counting[:, 0, :], before).then_inc(counting_ready, 1)
        link(dve.memset(zero[:, :], 0.0))
        dve.tensor_copy(scaT[:, :, :].rearrange("p t s -> p (t s)"), zero[:, 0:1].broadcast_to([P, TT * P])).then_inc(scaT_sb, 1)
        dve.tensor_copy(y_parts[:, :], zero[:, 0:1].broadcast_to([P, 1024])).then_inc(y_ready, 1)
        dve.memset(stats[:, 0, 0:1, :], 0.0).then_inc(hidT_sb, 1)
        dve.memset(stats[:, 1, 0:1, :], 0.0).then_inc(up_read, 1)

        dve.wait_ge(x_again_in, 16)
        for t in range(TT):
            for half in range(2):
                if 2 * t + half < 3:
                    dve.wait_ge(mixed_done, 2 * t + half + 1)
                else:
                    dve.wait_ge(pieces_used, N_MIX)
                cut = slice(half * 512, half * 512 + 512)
                dve.tensor_tensor(x2[:, t, cut], bank[2 + 2 * t + half][:, :], x_again[:, t, cut], ALU.add).then_inc(x2_sb, 1)
        for u in range(2):
            dve.wait_ge(x2T_done, u + 3)
            dve.tensor_copy(x2T[:, 4 * u:4 * u + 4, P:2 * P], bank[u][:, :].rearrange("p (c t) -> p c t", c=4))\
                .then_inc(x2T_sb, 1)
        for t in range(TT):
            dve.wait_ge(logit_parts_done, t + 1)
            dve.tensor_copy(logit_parts[:, t * P:(t + 1) * P], bank[4 - t][:, 0:P]).then_inc(logit_parts_sb, 1)
        rstd(2)

        dve.wait_ge(logits_done, 1)
        for t in range(TT):
            last = dve.scalar_tensor_tensor(logit[:, t, :], bank[5][:, t * E:(t + 1) * E], norm[:, 2, 6 + t:7 + t], b_rt,
                                            ALU.mult, ALU.add)
        link(last)
        dve.max(best[:, 0, :], logit[:, 0, :])
        link(dve.max(best[:, 1, :], logit[:, 1, :]))
        dve.tensor_scalar(small[:, 0:2], best[:, :, 0], -1.0, None, ALU.mult).then_inc(best_ready, 1)
        dve.max_index(best_u[:, 0, :], best[:, 0, :], logit[:, 0, :])
        link(dve.max_index(best_u[:, 1, :], best[:, 1, :], logit[:, 1, :]))
        link(dve.tensor_copy(best_i, best_u[:, :, :]))
        for k in range(TOPK):
            for t in range(TT):
                if k == 0:
                    last = dve.tensor_scalar(mask[:, t, :], slot_no[:, 0:E], best_i[:, t, 0:1], None, ALU.is_equal)
                else:
                    last = dve.scalar_tensor_tensor(mask[:, t, :], slot_no[:, 0:E], best_i[:, t, k:k + 1],
                                                    mask[:, t, :], ALU.is_equal, ALU.add)
            if k < TOPK - 1:
                link(last)
        last.then_inc(mask_sb, 1)

        dve.wait_ge(rank_done, 1)
        link(dve.scalar_tensor_tensor(rank, bank[4][:, 0:TT * E].rearrange("p (t e) -> p t e", t=TT), 1.0, mask[:, :, :],
                                      ALU.add, ALU.mult))
        link(dve.tensor_scalar(place[:, :, 0:E], rank, -1.0, None, ALU.add))
        def gather_matrix(s):
            for t in range(TT):
                last = dve.tensor_scalar(gat[:, t, :], slot_no[:, 0:SLOTS], place[:, t, bass.ds(s, 1)], None, ALU.is_equal)
            last.then_inc(gat_ready, 1)

        def scatter_matrix(s):
            for t in range(TT):
                last = dve.tensor_scalar(sca[:, t, :], slot_no, place[:, t, bass.ds(s, 1)], wexp[:, t, bass.ds(s, 1)],
                                         ALU.is_equal, ALU.mult)
            last.then_inc(sca_ready, 1)

        def bias_selector(s):
            dve.tensor_scalar(sel[:, :], half_of, pick[:, bass.ds(s, 1)], None, ALU.mult).then_inc(sel_ready, 1)

        gather_matrix(0)
        for b in range(1, PASSES):
            dve.tensor_scalar(place[:, :, b * E:(b + 1) * E], rank, -1.0 - SLOTS * b, None, ALU.add)

        link(dve.tensor_reduce(small[:, 6:7], bank[4][:, TT * E:(TT + 1) * E], AX.X, ALU.max))
        link(dve.tensor_scalar(small[:, 7:8], small[:, 6:7], float(SLOTS), None, ALU.is_gt))
        for b in range(2, PASSES):
            link(dve.scalar_tensor_tensor(small[:, 6 + b:7 + b], small[:, 6:7], float(SLOTS * b),
                                          small[:, 5 + b:6 + b], ALU.is_gt, ALU.add))
        dve.tensor_copy(more_i32[0:1, 0:1], small[0:1, 5 + PASSES:6 + PASSES]).then_inc(passes_ready, 1)
        dve.wait_ge(router_exp, 1)
        dve.wait_ge(mask_sb, 1)
        link(dve.tensor_tensor(elog, elog, mask[:, :, :], ALU.mult))
        link(dve.tensor_reduce(small[:, 2:4], elog, AX.X, ALU.add))
        link(dve.reciprocal(small[:, 4:6], small[:, 2:4]))
        for t in range(TT):
            for b in range(PASSES):
                last = dve.tensor_scalar(wexp[:, t, b * E:(b + 1) * E], elog[:, t, :], small[:, 4 + t:5 + t], None, ALU.mult)
        dve.memset(wexp[:, :, STEPS:], 0.0)
        last = dve.memset(place[:, :, STEPS:], -1.0)
        last.then_inc(weights_sb, 1)

        bias_selector(0)
        dve.wait_ge(weights_sb, 1)
        scatter_matrix(0)
        dve.wait_ge(gathered, 1)
        dve.tensor_tensor(xg, tr_ps[:, :].rearrange("p (c s) -> p c s", c=KC),
                          g_ffn.unsqueeze(2).broadcast_to([P, KC, SLOTS]), ALU.mult).then_inc(xg_sb, 1)

        more = dve.value_load(more_i32[0:1, 0:1], min_val=0, max_val=PASSES - 1)
        with dve.Fori(0, more * (E // 2) + E // 2) as i:
            for u in range(2):
                s = i * 2 + u
                dve.wait_ge(gathered, s + 1)
                gather_matrix(s + 1)
                dve.wait_ge(pieces_used, (s + 1) * KC + N_MIX)
                dve.tensor_scalar(g_sb, gate_ps[:, :], LIMIT, None, ALU.min).then_inc(g_ready, 1)
                dve.tensor_scalar(hid, lin_ps[:, :], LIMIT, -LIMIT, ALU.min, ALU.max).then_inc(up_read, 1)
                dve.wait_ge(g_ready, s + 1)
                dve.wait_ge(up_read, s + 2)
                dve.scalar_tensor_tensor(hid, hid, 1.0, g_sb, ALU.add, ALU.mult).then_inc(hid_half, 1)
                dve.wait_ge(hid_half, s + 1)
                dve.wait_ge(sig_ready, s + 1)
                dve.tensor_tensor(hid, hid, sg, ALU.mult).then_inc(hid_ready, 1)
                dve.wait_ge(w_slot_ready, s + 1)
                dve.wait_ge(scattered, s + 1)
                dve.tensor_scalar(scaT[:, :, :].rearrange("p t s -> p (t s)"), y_ps[:, 0:TT * P], 0.0, None, ALU.not_equal)\
                    .then_inc(scaT_sb, 1)
                bias_selector(s + 1)
                dve.wait_ge(gathered, s + 2)
                dve.tensor_tensor(xg, tr_ps[:, :].rearrange("p (c s) -> p c s", c=KC),
                                  g_ffn.unsqueeze(2).broadcast_to([P, KC, SLOTS]), ALU.mult).then_inc(xg_sb, 1)
                scatter_matrix(s + 1)
                dve.wait_ge(downs_used, (s + 1) * DRING)
                dve.wait_ge(y_high, s + 1)
                dve.scalar_tensor_tensor(y_parts[64:128, 0:512], y_ps[0:64, :], w_slot[0:64, :],
                                         y_parts[0:64, 0:512].bitcast(fp32), ALU.mult, ALU.subtract)
                dve.scalar_tensor_tensor(y_parts[0:64, 512:1024], y_ps[64:128, :], w_slot[64:128, :],
                                         y_parts[64:128, 512:1024].bitcast(fp32), ALU.mult, ALU.subtract)\
                    .then_inc(y_ready, 1)

        dve.wait_ge(final_gain_in, 16)
        for t in range(TT):
            dve.wait_ge(sq_done, 3 * TT + t + 1)
            at = norm[:, 3, 4 + t:5 + t]
            link(dve.tensor_scalar(at, norm[:, 3, 2 * t:2 * t + 1], norm[:, 3, 2 * t + 1:2 * t + 2], 1.0 / D, ALU.add, ALU.mult))
            dve.tensor_scalar(at, at, EPS, None, ALU.add).then_inc(mean_done, 1)
            dve.wait_ge(root_done, 4 + t)
            link(dve.reciprocal(at, norm[:, 3, 6 + t:7 + t]))
            for half in range(2):
                cut = slice(half * 512, half * 512 + 512)
                last = dve.scalar_tensor_tensor(x2[:, t, cut], acc[t][half][:, :], at, gain_out[:, cut], ALU.mult, ALU.mult)
            last.then_inc(fin_sb, 1)

    @block.tensor
    def _(pe):
        mm, transpose = pe.matmul, pe.transpose

        def parts(p, chunks):
            pe.wait_ge(w_low_ready, p + 1)
            return [w.rearrange("p (c n) -> p c n", c=chunks) for w in (w_high[p % 3][:, :], w_low[mixer_slot(p)][:, :])]

        def product(dst, lhsT, rhs, at_l, at_r, first, last):
            for n, (l, r) in enumerate(((0, 0), (0, 1), (1, 0))):
                ins = mm(dst, lhsT[l][at_l], rhs[r][at_r], start=first and n == 0, stop=last and n == 2)
            return ins

        def transposed(src, u, out_bank, done):
            t, half = u // 2, u % 2
            for c in range(4):
                last = transpose(out_bank[:, c * P:(c + 1) * P], src[:, t, (4 * half + c) * P:(4 * half + c + 1) * P], ident)
            last.then_inc(done, 1)

        pe.wait_ge(table_in, 16)
        mm(bank[3][0:ATT_H, 0:TOEP], table, hot, start=True, stop=True).then_inc(dist_done, 1)
        pe.wait_ge(rows_in, 16 * 2)
        transpose(bank[2][:, 0:60], rows, ident[0:60, 0:60]).then_inc(cols_done, 1)
        for u in range(4):
            pe.wait_ge(normed, u // 2 + 1)
            transposed(mem_nat, u, bank[4 + u], hT_done)

        def projection(u):
            if u >= 2:
                pe.wait_ge(proj_sb, u - 1)
            w = parts(u, KC)
            name, col = PROJ[u]
            src = (hT_high, hT_low) if name == "w_in" else (memT_high, memT_low)
            values = VA <= col < CB if name == "w_in" else col >= 512
            for k in range(2):
                dst, cut = bank[u % 2][:, k * 256:k * 256 + 256], slice(k * P, k * P + P)
                for c in range(KC):
                    narrow, wide = (slice(None), c, cut), (slice(None), c, slice(0, 256))
                    lhsT, rhs = (src, w) if values else (w, src)
                    last = product(dst, lhsT, rhs, narrow, wide, c == 0, c == KC - 1)
            last.then_inc(pieces_used, 1)

        def scores(hh):
            dst = bank[2 + hh % 2]
            if hh < ATT_H:
                if hh >= 2:
                    pe.wait_ge(att_scores_read, hh - 1)
                else:
                    pe.wait_ge(bias_sb, 3 + hh)
                q = qk[64 * (hh % 2):64 * (hh % 2) + 64, hh // 2, :]
                k = qk[64 * (hh % 2):64 * (hh % 2) + 64, 4 + hh // 2, :]
                mm(dst[:, 0:256], q[:, P:2 * P], k, start=True, stop=True)
                mm(dst[:, 256:384], q[:, 0:P], k[:, 0:P], start=True, stop=True).then_inc(scores_done, 1)
            else:
                if hh < ATT_H + 2:
                    pe.wait_ge(att_scores_read, hh - 1)
                else:
                    pe.wait_ge(exp_done, hh - 1)
                for t in range(TT):
                    last = mm(dst[:, t * 256:t * 256 + 256], qx[:, hh - ATT_H, t * P:(t + 1) * P], kx[:, hh - ATT_H, :],
                              start=True, stop=True)
                last.then_inc(scores_done, 1)

        def probs_transposed(hh):
            pe.wait_ge(probs_ready, hh + 1)
            if hh:
                pe.wait_ge(probsT_sb, hh)
            pr, dst = probs[hh % 2], bank[4]
            moves = ([(0, 256), (128, 0), (256, 128)] if hh < ATT_H else
                     [(k * 256 + t * P, t * 256 + k * P) for k in range(2) for t in range(TT)])
            for to, at in moves:
                last = transpose(dst[:, to:to + P], pr[:, at:at + P], ident)
            last.then_inc(probsT_done, 1)

        def values(hh):
            pe.wait_ge(probsT_sb, hh + 1)
            pT = probsT[hh % 2]
            u = hh // 2 if hh < ATT_H else hh - ATT_H // 2
            if u:
                pe.wait_ge(y_att_sb, u)
            if hh < ATT_H:
                dst = bank[5][64 * (hh % 2):64 * (hh % 2) + 64, 0:256]
                mm(dst, v_att[:, 0, 64 * hh:64 * hh + 64], pT[:, 0:256], start=True, stop=False)
                last = mm(dst[:, P:2 * P], v_att[:, 1, 64 * hh:64 * hh + 64], pT[:, 256:384], start=False, stop=True)
                if hh % 2:
                    last.then_inc(pv_done, 1)
            else:
                x = hh - ATT_H
                dst = bank[5][:, 0:256]
                for k in range(2):
                    last = mm(dst, vx[:, k, x * P:(x + 1) * P], pT[:, k * 256:k * 256 + 256], start=(k == 0), stop=(k == 1))
                last.then_inc(pv_done, 1)

        def heads(j):
            if 0 <= j < HEADS:
                scores(j)
            if 0 <= j - 2 < HEADS:
                probs_transposed(j - 2)
            if 0 <= j - 3 < HEADS:
                values(j - 3)

        pe.wait_ge(hT_parts, 4)
        for p in range(N_PROJ):
            if p == 4:
                pe.wait_ge(hT_parts, 8)
            projection(p)
            if p == 0:
                for u in range(4):
                    pe.wait_ge(normed, TT + u // 2 + 1)
                    transposed(x_nat, u, bank[4 + u], hT_done)
            if p in (3, 4):
                pe.wait_ge(bias_in, 16)
                pe.wait_ge(flip_in, 16)
                pe.wait_ge(cols_sb, 1)
                pe.wait_ge(dist_sb, 1)
                for j in range(2 * (p - 3), 2 * (p - 2)):
                    if j >= 2:
                        pe.wait_ge(bias_sb, j - 1)
                    mm(bank[2 + j % 2][:, :], flip, bias[:, 2 * j:2 * j + 2, :].rearrange("p h k -> p (h k)"),
                       start=True, stop=True).then_inc(bias_flipped, 1)
            heads(p - FIRST_HEAD)

        def gate_logits(n):
            w = parts(N_PROJ + 3 * (n // 2) + n % 2, KC)
            if n < 2:
                pe.wait_ge(proj_sb, N_PROJ - 1 + n)
            else:
                pe.wait_ge(gates_sb, n - 1)
            for k in range(2):
                for c in range(KC):
                    last = product(bank[n % 2][:, k * 256:k * 256 + 256], w, (hT_high, hT_low),
                                   (slice(None), c, slice(k * P, (k + 1) * P)), (slice(None), c, slice(0, S)),
                                   c == 0, c == KC - 1)
            last.then_inc(pieces_used, 1)

        def branch(g, second):
            b = GROUPS[g][0]
            w = parts(N_PROJ + 3 * g + 2, 4)
            y = {1: (y_conv_high, y_conv_low), 0: (y_att_high, y_att_low), 2: (y_x_high, y_x_low)}[b]
            if b == 1:
                pe.wait_ge(conv_parts, 2)
            else:
                pe.wait_ge(y_att_sb, ATT_H // 2 + (X_H if b == 2 else 0))
            if g:
                pe.wait_ge(merged_sb, 2 * g - 1 + second)
            for k in range(2):
                at = (2 * second + k) * P
                for c in range(4):
                    last = product(bank[6 + second][:, k * 256:k * 256 + 256], w, y,
                                   (slice(None), c, slice(at, at + P)), (slice(None), c, slice(0, S)), c == 0, c == 3)
            last.then_inc(pieces_used if second else branch_done, 1)

        for g in range(len(GROUPS)):
            gate_logits(2 * g)
            heads(ATT_H + 2 * g)
            gate_logits(2 * g + 1)
            branch(g, 0)
            heads(ATT_H + 2 * g + 1)
            branch(g, 1)

        pe.wait_ge(exp_done, HEADS)
        pe.wait_ge(probsT_sb, HEADS)
        pe.wait_ge(y_att_sb, ATT_H // 2 + X_H)
        for j in range(4):
            pe.wait_ge(merged_parts, 2 if j < 2 else 4)
            w = parts(N_MIX - 4 + j, 2)
            order = [(k, t, half) for k in range(2) for t in range(TT) for half in range(2)]
            if j == 3:
                order = [(k, t, half) for t in range(TT) for half in range(2) for k in range(2)]
            for n, (k, t, half) in enumerate(order):
                c = 2 * j + k
                last = product(bank[2 + 2 * t + half][:, :], (merged_high, merged_low), w,
                                              (slice(None), c, slice(t * P, (t + 1) * P)),
                                              (slice(None), k, slice(half * 512, half * 512 + 512)), c == 0, c == KC - 1)
                if j == 3 and n in (1, 3, 5):
                    last.then_inc(mixed_done, 1)
            last.then_inc(pieces_used, 1)

        def scatter(t, stop):
            for half in range(2):
                last = mm(acc[t][half][:, :], scaT[:, t, :], y_parts[:, half * 512:half * 512 + 512], start=False, stop=stop)
            return last

        pe.wait_ge(merged_sb, 12)
        pe.wait_ge(gates_sb, 12)
        for u in range(4):
            pe.wait_ge(x2_sb, u + 1)
            transposed(x2, u, bank[(6, 7, 0, 1)[u]], x2T_done)
        pe.wait_ge(w_rt_ready, 1)
        for t in range(TT):
            pe.wait_ge(x2T_sb if t else x2T_copied, 2)
            for c in range(KC):
                at = 32 * (c % 4)
                last = mm(bank[4 - t][at:at + 32, 0:P], w_rt[:, c, :], x2T[:, c, t * P:(t + 1) * P],
                          start=(c < 4), stop=(c >= 4))
            last.then_inc(logit_parts_done, 1)
        for t in range(TT):
            pe.wait_ge(logit_parts_sb, t + 1)
            last = mm(bank[5][:, t * E:(t + 1) * E], logit_parts[:, t * P:(t + 1) * P], pick[:, 0:E], start=True, stop=True)
        last.then_inc(logits_done, 1)
        for t in range(TT):
            for half in range(2):
                mm(acc[t][half][:, :], ident, x2[:, t, half * 512:half * 512 + 512], start=True, stop=False)
        pe.wait_ge(counting_ready, 1)
        pe.wait_ge(mask_sb, 1)
        triangle, ones = counting[:, 0, :], counting[:, 1, :]
        mm(bank[4][:, 0:E], triangle, mask[:, 0, :], start=True, stop=True)
        mm(bank[4][:, E:2 * E], ones, mask[:, 0, :], start=True, stop=False)
        mm(bank[4][:, E:2 * E], triangle, mask[:, 1, :], start=False, stop=True)
        mm(bank[4][:, 2 * E:3 * E], ones, mask[:, 0, :], start=True, stop=False)
        mm(bank[4][:, 2 * E:3 * E], ones, mask[:, 1, :], start=False, stop=True).then_inc(rank_done, 1)

        def gather(s):
            pe.wait_ge(gat_ready, s + 1)
            for c in range(KC):
                for t in range(TT):
                    last = mm(tr_ps[:, c * SLOTS:(c + 1) * SLOTS], h2[:, t, c * P:(c + 1) * P], gat[:, t, :],
                              start=(t == 0), stop=(t == TT - 1))
            last.then_inc(gathered, 1)

        pe.wait_ge(h2_sb, TT)
        gather(0)
        pe.wait_ge(weights_sb, 1)
        for t in range(TT):
            last = transpose(bank[7][0:E, t * P:(t + 1) * P], wexp[:, t, 0:E], ident)
        last.then_inc(wexpT_done, 1)
        pe.wait_ge(wexpT_sb, 1)
        more = pe.value_load(more_i32[0:1, 0:1], min_val=0, max_val=PASSES - 1)
        with pe.Fori(0, more * (E // 2) + E // 2) as i:
            for u in range(2):
                s = i * 2 + u
                slot0 = 8 if u == 0 else 0
                pe.wait_ge(sel_ready, s + 1)
                pe.wait_ge(up_read, s + 1)
                for k, ps in enumerate((gate_ps, lin_ps)):
                    mm(ps[:, :], sel[:, :], b_parts[:, k * 512:k * 512 + 512], start=True, stop=False)
                pe.wait_ge(xg_sb, s + 1)
                for c in range(KC):
                    pe.wait_ge(piece_in[slot0 + c], i * 16 + 16 * (loads_before(slot0 + c) + 1))
                    for k, ps in enumerate((gate_ps, lin_ps)):
                        for half in range(2):
                            last = mm(ps[64 * half:64 * half + 64, :], xg[:, c, :],
                                      ring[:, slot0 + c, k * F + half * 512:k * F + half * 512 + 512],
                                      start=False, stop=(c == KC - 1))
                    last.then_inc(pieces_used, 1)
                pe.wait_ge(y_ready, s + 1)
                pe.wait_ge(scaT_sb, s + 1)
                scatter(0, False)
                scatter(1, False).then_inc(scattered, 1)
                pe.wait_ge(sca_ready, s + 1)
                for t in range(TT):
                    last = transpose(y_ps[:, t * P:(t + 1) * P], sca[:, t, :], ident)
                last.then_inc(scaT_done, 1)
                pe.wait_ge(hidT_sb, s + 1)
                gather(s + 1)
                pe.wait_ge(hid_ready, s + 1)
                pe.wait_ge(xg_sb, s + 2)
                for c in range(4):
                    last = transpose(tr_ps[:, c * P:(c + 1) * P], hid[:, c * P:(c + 1) * P], ident)
                last.then_inc(hidT_done, 1)
                pe.wait_ge(hidT_sb, s + 2)
                pe.wait_ge(scaT_sb, s + 2)
                pe.wait_ge(w_slot_ready, s + 1)
                for c in range(KC):
                    if c % 2 == 0:
                        pe.wait_ge(down_in[c // 2], (s + 1) * 16)
                    lhsT = hidT[:, (c % 4) * P + 64 * (c // 4):(c % 4) * P + 64 * (c // 4) + 64]
                    for half in range(2):
                        at = (c % 2) * D + half * 512
                        last = mm(y_ps[64 * half:64 * half + 64, :], lhsT, dring[:, c // 2, at:at + 512],
                                  start=(c == 0), stop=(c == KC - 1))
                    if c % 2:
                        last.then_inc(downs_used, 1)
        pe.wait_ge(b_down_in, 16)
        for t in range(TT):
            for half in range(2):
                mm(acc[t][half][:, :], wexpT[:, t * P:(t + 1) * P], b_down[:, half * 512:half * 512 + 512],
                   start=False, stop=False)
        pe.wait_ge(y_ready, more * E + (E + 1))
        pe.wait_ge(scaT_sb, more * E + (E + 1))
        for t in range(TT):
            scatter(t, True).then_inc(acc_done, 1)



_INS = ["x", "mem", "rel_bias", "norm_mix_g", "w_in", "b_gate", "conv_w", "norm_mem_g", "w_mem_kv",
        "w_br_att", "w_br_conv", "w_br_xatt", "w_out", "norm_ffn_g", "w_router", "b_router",
        "w_gu", "b_gu", "w_down", "b_down", "norm_final_g"]


def kernel(**inputs):
    import numpy as _np
    import concourse.bacc as _bacc
    from concourse import mybir as _mybir
    from concourse.bass_utils import run_bass_kernel_spmd as _run

    nc = _bacc.Bacc("TRN2", target_bir_lowering=False, num_devices=1)
    given = {name: _np.ascontiguousarray(inputs[name]) for name in _INS}
    given["consts"], hot = shape_constants()
    given["rows"] = _np.concatenate([given.pop(k).reshape(-1, P) for k in
                                     ("norm_mix_g", "norm_mem_g", "norm_ffn_g", "b_gate", "conv_w")])
    future = _np.full((1, ATT_H), NEG, _np.float32)
    given["table_hot"] = _np.concatenate([_np.concatenate([given.pop("rel_bias"), future]), hot], axis=1)
    rows = given["b_gu"].reshape(E, 2, 2, F // 2).transpose(2, 0, 1, 3).reshape(2 * E, F)
    given["b_gu"] = _np.concatenate([rows, rows])
    arrays, args = {}, {}
    for name, value in given.items():
        arrays[f"in_{name}_dram"] = value
        args[name] = nc.dram_tensor(f"in_{name}_dram", value.shape, _mybir.dt.from_np(value.dtype), kind="ExternalInput").ap()
    out = nc.dram_tensor("out_0_dram", (1, S, D), _mybir.dt.float32, kind="ExternalOutput").ap()
    scratch = nc.dram_tensor("bias_scratch", [ATT_H, 384], _mybir.dt.float32, kind="Internal").ap()
    trunk_layer(nc, args, out, scratch)
    r = _run(nc, [arrays], core_ids=[0])
    return r.results[0]["out_0_dram"]
```
